# Optimizing a Trainium2 kernel written in Bass

```python
import math
import jax, jax.numpy as jnp
from jax import lax
import numpy as np

D_MODEL = 1024
BATCH = 1
SEQ = 512
DEPTH = 2

GRID_W = 64
CTX_LEN = 256
EPS = 1e-6

GDN_HEADS = 4
GDN_DK = 128
GDN_DV = 128
GDN_CONV = 5
GDN_CHUNK = 64
CMLP_GROUPS = 4
CMLP_CH = 128
CMLP_CHUNK = 128
DA_HEADS = 4
DA_DH = 64
DA_DV = 2 * DA_DH
DA_QBLOCK = 128
ROPE_BASE = 10000.0
PEER_HEADS = 8
PEER_NKEYS = 128
PEER_EXPERTS = PEER_NKEYS * PEER_NKEYS
PEER_QDIM = 256
PEER_TOPK = 16
PEER_TBLOCK = 128

MIX_A = GDN_HEADS * GDN_DV
MIX_B = CMLP_GROUPS * CMLP_CH
MIX_C = DA_HEADS * DA_DV
GDN_QKV = GDN_HEADS * (2 * GDN_DK + GDN_DV)

IN_SIZES = (
    GDN_QKV,
    GDN_HEADS * GDN_DV,
    4 * GDN_HEADS,
    2 * MIX_B,
    DA_HEADS * 2 * DA_DH,
    DA_HEADS * 2 * DA_DH,
    DA_HEADS * DA_DV,
    3 * D_MODEL,
)

kernel_name = 'hybrid_gdn_chunkmlp_diffattn_peer'

def _split(t, sizes):
    out, start = [], 0
    for s in sizes:
        out.append(t[..., start:start + s])
        start += s
    return out

def _rmsnorm(x, g):
    xf = x.astype(jnp.float32)
    y = xf * lax.rsqrt(jnp.mean(xf * xf, axis=-1, keepdims=True) + EPS)
    return (y * g.astype(jnp.float32)).astype(x.dtype)

def _l2norm(x):
    xf = x.astype(jnp.float32)
    return xf * lax.rsqrt(jnp.sum(xf * xf, axis=-1, keepdims=True) + EPS)

def _modulate(h, shift, scale):
    return h * (1.0 + scale) + shift

def _short_conv(x, w):
    k = w.shape[0]
    return lax.conv_general_dilated(x, w[:, None, :].astype(x.dtype), window_strides=(1,),
                                    padding=[(k // 2, k // 2)], dimension_numbers=('NWC', 'WIO', 'NWC'),
                                    feature_group_count=x.shape[-1])

def _gdn_prep(qkv, ba, conv_w, a_log, dt_bias):
    b, l, _ = qkv.shape
    qkv = jax.nn.silu(_short_conv(qkv, conv_w))
    q, k, v = _split(qkv, (GDN_HEADS * GDN_DK, GDN_HEADS * GDN_DK, GDN_HEADS * GDN_DV))
    q = _l2norm(q.reshape(b, l, GDN_HEADS, GDN_DK)) * GDN_DK ** -0.5
    k = _l2norm(k.reshape(b, l, GDN_HEADS, GDN_DK))
    v = v.reshape(b, l, GDN_HEADS, GDN_DV).astype(jnp.float32)
    ba = ba.astype(jnp.float32).reshape(b, l, 2, 2, GDN_HEADS)
    beta = jax.nn.sigmoid(ba[:, :, 0])
    g = -jnp.exp(a_log.astype(jnp.float32)) * jax.nn.softplus(ba[:, :, 1] + dt_bias.astype(jnp.float32))
    return q, k, v, g, beta

def _gated_delta_chunked(q, k, v, g, beta, s0):
    b, l, h, dk = q.shape
    dv = v.shape[-1]
    c = GDN_CHUNK
    n = l // c

    def chunks(t):
        return jnp.moveaxis(t.reshape(b, n, c, h, *t.shape[3:]), 3, 1)

    qc, kc, vc = chunks(q), chunks(k), chunks(v)
    gc = jnp.cumsum(chunks(g), axis=-1)
    bc = chunks(beta)
    incl = jnp.tril(jnp.ones((c, c), dtype=bool))
    strict = jnp.tril(jnp.ones((c, c), dtype=bool), -1)
    gdiff = gc[..., :, None] - gc[..., None, :]
    decay = jnp.where(incl, jnp.exp(jnp.where(incl, gdiff, 0.0)), 0.0)
    kk = jnp.einsum('bhncd,bhnsd->bhncs', kc, kc)
    lower = jnp.where(strict, kk * decay * bc[..., :, None], 0.0)
    eye = jnp.eye(c, dtype=jnp.float32)
    t_inv = lax.linalg.triangular_solve(eye + lower, jnp.broadcast_to(eye, lower.shape),
                                        left_side=True, lower=True, unit_diagonal=True)
    u = jnp.einsum('bhncs,bhnsd->bhncd', t_inv, vc * bc[..., None])
    w = jnp.einsum('bhncs,bhnsd->bhncd', t_inv, kc * (bc * jnp.exp(gc))[..., None])
    qk = jnp.einsum('bhncd,bhnsd->bhncs', qc, kc) * decay
    q_dec = qc * jnp.exp(gc)[..., None]
    k_dec = kc * jnp.exp(gc[..., -1:] - gc)[..., None]
    g_last = jnp.exp(gc[..., -1])

    def step(state, xs):
        u_i, w_i, qk_i, qd_i, kd_i, gl_i = xs
        v_new = u_i - jnp.einsum('bhcd,bhde->bhce', w_i, state)
        o_i = jnp.einsum('bhcd,bhde->bhce', qd_i, state) + jnp.einsum('bhcs,bhse->bhce', qk_i, v_new)
        state = state * gl_i[..., None, None] + jnp.einsum('bhcd,bhce->bhde', kd_i, v_new)
        return state, o_i

    xs = tuple(jnp.moveaxis(t, 2, 0) for t in (u, w, qk, q_dec, k_dec, g_last))
    s_fin, o = lax.scan(step, s0, xs)
    o = jnp.transpose(o, (1, 0, 3, 2, 4)).reshape(b, l, h, dv)
    return o, s_fin

def _gdn_dir(prep, d, s0):
    q, k, v, g, beta = prep
    g, beta = g[:, :, d], beta[:, :, d]
    if d == 1:
        q, k, v, g, beta = (jnp.flip(t, axis=1) for t in (q, k, v, g, beta))
    o, s = _gated_delta_chunked(q, k, v, g, beta, s0)
    if d == 1:
        o = jnp.flip(o, axis=1)
    return o, s

def _gdn_out(o, z, norm_g):
    b, l = z.shape[:2]
    zz = z.reshape(b, l, GDN_HEADS, GDN_DV).astype(jnp.float32)
    y = _rmsnorm(o, norm_g) * jax.nn.silu(zz)
    return y.reshape(b, l, MIX_A).astype(z.dtype)

def _chunk_mlp(uv, v_norm_g, w_s, b_s):
    b, l, _ = uv.shape
    u, v = jnp.split(jax.nn.gelu(uv), 2, axis=-1)
    v = _rmsnorm(v, v_norm_g).reshape(b, l // CMLP_CHUNK, CMLP_CHUNK, CMLP_GROUPS, CMLP_CH)
    sv = jnp.einsum('gpq,bnqgc->bnpgc', w_s, v) + b_s.T[:, :, None]
    return u * sv.reshape(b, l, MIX_B)

def _axial_rope(rows):
    r, col = jnp.meshgrid(jnp.arange(rows), jnp.arange(GRID_W), indexing='ij')
    n_freq = DA_DH // 4
    inv = ROPE_BASE ** (-jnp.arange(n_freq, dtype=jnp.float32) / n_freq)
    ang = jnp.concatenate([r.reshape(-1, 1).astype(jnp.float32) * inv,
                           col.reshape(-1, 1).astype(jnp.float32) * inv], axis=-1)
    return jnp.cos(ang), jnp.sin(ang)

def _rope(x, cos, sin):
    half = DA_DH // 2
    x1, x2 = x[..., :half], x[..., half:]
    cs, sn = cos[:, None, None, :], sin[:, None, None, :]
    return jnp.concatenate([x1 * cs - x2 * sn, x1 * sn + x2 * cs], axis=-1).astype(x.dtype)

def _da_qk(t, g, rope):
    b, l, _ = t.shape
    t = _rmsnorm(t.reshape(b, l, DA_HEADS, 2, DA_DH), g)
    if rope is not None:
        t = _rope(t, *rope)
    return jnp.transpose(t, (0, 2, 3, 1, 4))

def _da_v(t):
    b, l, _ = t.shape
    return jnp.transpose(t.reshape(b, l, DA_HEADS, DA_DV), (0, 2, 1, 3))

def _da_attend(q, k_all, v_all, lam):
    s = jnp.einsum('bhiqd,bhikd->bhiqk', q, k_all, preferred_element_type=jnp.float32) * DA_DH ** -0.5
    p = jax.nn.softmax(s, axis=-1)
    a = p[:, :, 0] - lam * p[:, :, 1]
    return jnp.einsum('bhqk,bhkd->bhqd', a.astype(v_all.dtype), v_all)

def _da_out(o, subln_g, lam_init):
    b, h, l, dv = o.shape
    o = _rmsnorm(o, subln_g) * (1.0 - lam_init)
    return jnp.transpose(o, (0, 2, 1, 3)).reshape(b, l, MIX_C)

def _merge(oa, ob, oc, gates, wa, wb, wc, wo):
    ga, gb, gc = jnp.split(jax.nn.sigmoid(gates), 3, axis=-1)
    y = ga * (oa @ wa) + gb * (ob @ wb) + gc * (oc @ wc)
    return y @ wo

def _peer(h, w_q, subkeys, u_tab, v_tab):
    t, d = h.shape
    q = (h @ w_q).reshape(t, PEER_HEADS, 2, PEER_QDIM // 2)
    s = jnp.einsum('thid,hind->thin', q, subkeys, preferred_element_type=jnp.float32)
    s_top, i_top = lax.top_k(s, PEER_TOPK)
    kk = PEER_TOPK * PEER_TOPK
    cand = (s_top[:, :, 0, :, None] + s_top[:, :, 1, None, :]).reshape(t, PEER_HEADS, kk)
    cand_idx = (i_top[:, :, 0, :, None] * PEER_NKEYS + i_top[:, :, 1, None, :]).reshape(t, PEER_HEADS, kk)
    best, pos = lax.top_k(cand, PEER_TOPK)
    idx = jnp.take_along_axis(cand_idx, pos, axis=-1)
    gate = jax.nn.softmax(best, axis=-1)
    nb = t // PEER_TBLOCK

    def block(args):
        hb, ib, gb = args
        act = jax.nn.gelu(jnp.einsum('td,thkd->thk', hb, u_tab[ib], preferred_element_type=jnp.float32))
        return jnp.einsum('thk,thkd->td', (gb * act).astype(v_tab.dtype), v_tab[ib])

    out = lax.map(block, (h.reshape(nb, PEER_TBLOCK, d),
                          idx.reshape(nb, PEER_TBLOCK, PEER_HEADS, PEER_TOPK),
                          gate.reshape(nb, PEER_TBLOCK, PEER_HEADS, PEER_TOPK)))
    return out.reshape(t, d)

def setup_inputs(seed: int = 0) -> dict:
    key = jax.random.key(seed)
    ks = jax.random.split(key, 28)
    D = D_MODEL
    f32 = jnp.float32

    def nrm(k, shape, std):
        return jax.random.normal(k, shape, f32) * std

    def gain(k, shape):
        return 1.0 + 0.02 * jax.random.normal(k, shape, f32)

    in_cols = sum(IN_SIZES)
    dt = jnp.exp(jax.random.uniform(ks[10], (DEPTH, 2, GDN_HEADS), dtype=f32,
                                    minval=math.log(1e-3), maxval=math.log(1e-1)))
    return {
        'x': nrm(ks[0], (BATCH, SEQ, D), 1.0),
        'c': nrm(ks[1], (BATCH, D), 1.0),
        'ctx': nrm(ks[2], (BATCH, CTX_LEN, D), 1.0),
        'c_ctx': nrm(ks[3], (D,), 1.0),
        'w_mod': nrm(ks[4], (DEPTH, D, 6 * D), 0.5 * D ** -0.5),
        'b_mod': nrm(ks[5], (DEPTH, 6 * D), 0.02),
        'norm1_g': gain(ks[6], (DEPTH, D)),
        'w_in': nrm(ks[7], (DEPTH, D, in_cols), D ** -0.5),
        'gdn_conv_w': nrm(ks[8], (DEPTH, GDN_CONV, GDN_QKV), GDN_CONV ** -0.5),
        'gdn_a_log': jnp.log(jax.random.uniform(ks[9], (DEPTH, 2, GDN_HEADS), dtype=f32, minval=1.0, maxval=16.0)),
        'gdn_dt_bias': dt + jnp.log(-jnp.expm1(-dt)),
        'gdn_out_norm_g': gain(ks[11], (DEPTH, GDN_DV)),
        'cmlp_v_norm_g': gain(ks[12], (DEPTH, MIX_B)),
        'cmlp_w_s': nrm(ks[13], (DEPTH, CMLP_GROUPS, CMLP_CHUNK, CMLP_CHUNK), CMLP_CHUNK ** -0.5),
        'cmlp_b_s': gain(ks[14], (DEPTH, CMLP_GROUPS, CMLP_CHUNK)),
        'da_q_norm_g': gain(ks[15], (DEPTH, DA_DH)),
        'da_k_norm_g': gain(ks[16], (DEPTH, DA_DH)),
        'da_lambda': nrm(ks[17], (DEPTH, 4, DA_DH), 0.1),
        'da_subln_g': gain(ks[18], (DEPTH, DA_DV)),
        'w_branch_a': nrm(ks[19], (DEPTH, MIX_A, D), MIX_A ** -0.5),
        'w_branch_b': nrm(ks[20], (DEPTH, MIX_B, D), MIX_B ** -0.5),
        'w_branch_c': nrm(ks[21], (DEPTH, MIX_C, D), MIX_C ** -0.5),
        'w_out': nrm(ks[22], (DEPTH, D, D), D ** -0.5),
        'norm2_g': gain(ks[23], (DEPTH, D)),
        'peer_w_q': nrm(ks[24], (DEPTH, D, PEER_HEADS * PEER_QDIM), D ** -0.5),
        'peer_subkeys': nrm(ks[25], (DEPTH, PEER_HEADS, 2, PEER_NKEYS, PEER_QDIM // 2), (PEER_QDIM // 2) ** -0.5),
        'peer_u': nrm(ks[26], (DEPTH, PEER_EXPERTS, D), D ** -0.5),
        'peer_v': nrm(ks[27], (DEPTH, PEER_EXPERTS, D), 1.0),
    }

def reference(x, c, ctx, c_ctx, w_mod, b_mod, norm1_g, w_in, gdn_conv_w, gdn_a_log, gdn_dt_bias,
              gdn_out_norm_g, cmlp_v_norm_g, cmlp_w_s, cmlp_b_s, da_q_norm_g, da_k_norm_g, da_lambda,
              da_subln_g, w_branch_a, w_branch_b, w_branch_c, w_out, norm2_g, peer_w_q, peer_subkeys,
              peer_u, peer_v):
    b, L, d = x.shape
    lc = ctx.shape[1]
    rows = L // GRID_W
    rope = _axial_rope(rows)
    silu_c = jax.nn.silu(c)[:, None, :]
    silu_cc = jax.nn.silu(c_ctx)[None, None, :]
    n_qb = L // DA_QBLOCK
    for l in range(DEPTH):
        last = l == DEPTH - 1
        lam_init = 0.8 - 0.6 * math.exp(-0.3 * l)
        mx = jnp.split(silu_c @ w_mod[l] + b_mod[l], 6, axis=-1)
        mc = jnp.split(silu_cc @ w_mod[l] + b_mod[l], 6, axis=-1)

        hx = _modulate(_rmsnorm(x, norm1_g[l]), mx[0], mx[1])
        hc = _modulate(_rmsnorm(ctx, norm1_g[l]), mc[0], mc[1])
        px = _split(hx @ w_in[l], IN_SIZES)
        pc = _split(hc @ w_in[l], IN_SIZES)

        prep_x = _gdn_prep(px[0], px[2], gdn_conv_w[l], gdn_a_log[l], gdn_dt_bias[l])
        prep_c = _gdn_prep(pc[0], pc[2], gdn_conv_w[l], gdn_a_log[l], gdn_dt_bias[l])
        s_zero = jnp.zeros((b, GDN_HEADS, GDN_DK, GDN_DV), jnp.float32)
        oa_x, oa_c = 0.0, 0.0
        for dirn in range(2):
            o_c, s_c = _gdn_dir(prep_c, dirn, s_zero)
            o_x, _ = _gdn_dir(prep_x, dirn, s_c)
            oa_x = oa_x + o_x
            if not last:
                oa_c = oa_c + o_c
        ya_x = _gdn_out(oa_x, px[1], gdn_out_norm_g[l])

        yb_x = _chunk_mlp(px[3], cmlp_v_norm_g[l], cmlp_w_s[l], cmlp_b_s[l])

        lam_p = da_lambda[l].astype(jnp.float32)
        lam = jnp.exp(jnp.sum(lam_p[0] * lam_p[1])) - jnp.exp(jnp.sum(lam_p[2] * lam_p[3])) + lam_init
        qx = _da_qk(px[4], da_q_norm_g[l], rope)
        kx = _da_qk(px[5], da_k_norm_g[l], rope)
        vx = _da_v(px[6])
        kc = _da_qk(pc[5], da_k_norm_g[l], None)
        vc = _da_v(pc[6])
        k_all = jnp.concatenate([kc, kx], axis=3)
        v_all = jnp.concatenate([vc, vx], axis=2)
        q_blocks = jnp.moveaxis(qx.reshape(b, DA_HEADS, 2, n_qb, DA_QBLOCK, DA_DH), 3, 0)
        o_blocks = lax.map(lambda qb: _da_attend(qb, k_all, v_all, lam), q_blocks)
        ox = jnp.moveaxis(o_blocks, 0, 2).reshape(b, DA_HEADS, L, DA_DV)
        yc_x = _da_out(ox, da_subln_g[l], lam_init)

        mix_x = _merge(ya_x, yb_x, yc_x, px[7], w_branch_a[l], w_branch_b[l], w_branch_c[l], w_out[l])
        if not last:
            ya_c = _gdn_out(oa_c, pc[1], gdn_out_norm_g[l])
            yb_c = _chunk_mlp(pc[3], cmlp_v_norm_g[l], cmlp_w_s[l], cmlp_b_s[l])
            qc = _da_qk(pc[4], da_q_norm_g[l], None)
            yc_c = _da_out(_da_attend(qc, kc, vc, lam), da_subln_g[l], lam_init)
            mix_c = _merge(ya_c, yb_c, yc_c, pc[7], w_branch_a[l], w_branch_b[l], w_branch_c[l], w_out[l])
            ctx = ctx + mc[2] * mix_c
        x = x + mx[2] * mix_x

        hx = _modulate(_rmsnorm(x, norm2_g[l]), mx[3], mx[4])
        if last:
            fx = _peer(hx.reshape(b * L, d), peer_w_q[l], peer_subkeys[l], peer_u[l], peer_v[l]).reshape(b, L, d)
        else:
            hc = _modulate(_rmsnorm(ctx, norm2_g[l]), mc[3], mc[4])
            f = _peer(jnp.concatenate([hx.reshape(b * L, d), hc.reshape(b * lc, d)], axis=0),
                      peer_w_q[l], peer_subkeys[l], peer_u[l], peer_v[l])
            fx = f[:b * L].reshape(b, L, d)
            ctx = ctx + mc[5] * f[b * L:].reshape(b, lc, d)
        x = x + mx[5] * fx
    return x


_drawn_inputs = setup_inputs


def setup_inputs(seed=0):
    import zlib

    import numpy as np

    out = dict(_drawn_inputs(seed))
    spreads = {}
    factors = {'gdn_out_norm_g': 3.456,
     'cmlp_v_norm_g': 3.425,
     'cmlp_b_s': 3.373,
     'da_q_norm_g': 5.114,
     'da_k_norm_g': 4.659,
     'da_subln_g': 3.126}
    for name, (base, spread) in spreads.items():
        noise = np.random.default_rng([zlib.crc32(name.encode()), seed]).standard_normal(out[name].shape)
        drawn = base * np.exp(spread * noise) if base else spread * noise
        out[name] = __import__('jax').numpy.asarray(drawn.astype(out[name].dtype))
    for name, factor in factors.items():
        out[name] = (out[name] * factor).astype(out[name].dtype)
    return out
```

```python
import math
from contextlib import ExitStack

import numpy as np

import concourse.bass as bass
from concourse import mybir

F32 = mybir.dt.float32
U32 = mybir.dt.uint32
ALU = mybir.AluOpType
ACT = mybir.ActivationFunctionType
AX = mybir.AxisListType.X

P = 128
D = 1024
KD = D // P
LC, LX = 256, 512
T = LC + LX
TILES, CTILES = T // P, LC // P
EPS = 1e-6
DEPTH = 2
HEADS = 4
DH = 64
PH, TOPK, NKEYS = 8, 16, 128
PICKS = PH * TOPK
EXPERTS = NKEYS * NKEYS
LEVELS = 7
C_QKV, C_Z, C_BA, C_U, C_V, C_Q, C_K, C_DV, C_G = 0, 1536, 2048, 2064, 2576, 3088, 3600, 4112, 4624
PAD = 2
CW = LC + LX + 6 * PAD - 4
KIND_RANGE = ((LC, T, 0), (0, LC, 1))
BATCH = 8


def constants():
    i = np.arange(P)
    ident = np.eye(P, dtype=np.float32)
    upper = (i[:, None] <= i[None, :]).astype(np.float32)
    masks = np.zeros((P, 2, LEVELS, P), np.float32)
    for lv in range(LEVELS):
        s = 1 << lv
        low = (i[:, None] // s == i[None, :] // s + 1) & (i[:, None] // (2 * s) == i[None, :] // (2 * s))
        masks[:, 0, lv] = low
        masks[:, 1, lv] = low.T
    perm = np.zeros((P, P), np.float32)
    for b in (0, DH):
        for d in range(DH // 2):
            perm[b + d + DH // 2, b + d] = -1.0
            perm[b + d, b + d + DH // 2] = 1.0
    blockones = (i[:, None] // DH == i[None, :] // DH).astype(np.float32)
    sel = np.zeros((P, 8, P), np.float32)
    for j in range(8):
        sel[j, j] = 1.0
    inv = (10000.0 ** (-np.arange(DH // 4, dtype=np.float32) / np.float32(DH // 4))).astype(np.float32)
    t = np.arange(LX)
    ang = np.concatenate([(t // 64).astype(np.float32)[:, None] * inv,
                          (t % 64).astype(np.float32)[:, None] * inv], axis=-1)
    ang = np.tile(ang.T, (4, 1))
    cols = [("ident", ident), ("upper", upper), ("lower", upper.T), ("perm", perm), ("blockones", blockones),
            ("ident4", np.tile(ident, (1, HEADS))), ("masks", masks.reshape(P, -1)), ("sel", sel.reshape(P, -1)),
            ("cos", np.cos(ang)), ("sin", np.sin(ang)), ("ones", np.ones((P, P))),
            ("iota", np.tile(np.arange(TOPK), (P, 1)))]
    at, n = {}, 0
    for name, a in cols:
        at[name] = (n, a.shape[1])
        n += a.shape[1]
    return np.concatenate([np.asarray(a, np.float32) for _, a in cols], axis=1), at


def spans(lo):
    return ((0, LC), (LC, T)) if lo < LC else ((LC, T),)


class Steps:

    def __init__(self, eng, sem):
        self.eng, self.sem, self.n, self.off = eng, sem, 0, None

    def __call__(self, instruction):
        instruction.then_inc(self.sem, 1)
        self.n += 1

    def loop(self, i, per):
        self.off, self.n0, self.per = i * per, self.n, per

    def end(self, trips):
        assert self.n - self.n0 == self.per, (self.n - self.n0, self.per)
        self.n, self.off = self.n0 + self.per * trips, None

    def settle(self, back=0, apart=False):
        if self.off is None:
            self.eng.wait_ge(self.sem, self.n - back)
        else:
            self.eng.wait_ge(self.sem, self.off + (self.n - back))
            if apart:
                self.eng.nop(nofuse=True)


def hold(eng, sem, value):
    eng.wait_ge(sem, value)
    eng.nop(nofuse=True)


def over(ap, n):
    return ap.rearrange("p (o c) -> p o c", o=1).broadcast_to([ap.shape[0], n, ap.shape[1]])


def each(ap, n):
    return ap.rearrange("p (c o) -> p c o", o=1).broadcast_to([ap.shape[0], ap.shape[1], n])


class Stage:

    def __init__(self, k):
        self.k, self.used = k, 0

    def __enter__(self):
        self.st = ExitStack()
        self.st.__enter__()
        return self

    def sb(self, name, shape, dt=F32):
        self.k.serial += 1
        return self.st.enter_context(self.k.nc.sbuf_tensor(f"{name}_{self.k.serial}", shape, dt))

    def signals(self, n):
        self.used += n
        return self.k.sems[self.used - n:self.used]

    def __exit__(self, *a):
        self.st.__exit__(*a)
        first = self.k.sems[0].num
        self.k.nc.all_engine_barrier(sems_to_clear=range(first, first + self.used))


class Kernel:
    def __init__(self, nc, a, out, st):
        self.nc, self.a, self.out, self.serial = nc, a, out, 0
        self.sems = [nc.alloc_semaphore(f"stage_signal_{i}") for i in range(40)]
        assert [x.num for x in self.sems] == list(range(self.sems[0].num, self.sems[0].num + 40))

        self.gathered = [nc.alloc_semaphore(f"gathered_{j}") for j in range(BATCH)]
        self.gathered_count = 0

        def sb(name, shape, dt=F32):
            return st.enter_context(nc.sbuf_tensor(name, shape, dt))
        table, self.at = constants()
        self.const_dram = nc.inline_tensor(table)
        self.consts = sb("consts", [P, table.shape[1]])
        self.xT = sb("xT", [P, KD, T])
        self.hT = sb("hT", [P, KD, T])
        self.sT = sb("sT", [P, KD, 2])
        self.modT = sb("modT", [P, 6 * KD, 2])
        self.gain1 = sb("gain1", [P, KD, 2])
        self.gain2 = sb("gain2", [P, KD, 2])
        self.cols = sb("cols", [P, 4])
        self.eps = sb("eps", [P, 4 + DEPTH])
        self.ps = st.enter_context(nc.psum_tensor("ps", [P, 4, 2 * 512], F32))

    def c(self, name):
        at, n = self.at[name]
        return self.consts[:, at:at + n]

    def setup(self):
        nc, a, ps = self.nc, self.a, self.ps
        with Stage(self) as s:
            consts_in, c_in, x_in, turned, copied_even, copied_odd = s.signals(6)
            xn = s.sb("xn", [P, TILES, D])
            cT = s.sb("cT", [P, KD, 2])
            with nc.Block() as block:
                @block.sync
                def _(sp):
                    sp.dma_start(self.consts[:, :], self.const_dram[:, :]).then_inc(consts_in, 16)
                    sp.dma_start(xn[:, 0:CTILES, :], a["ctx"].rearrange("o (t p) d -> p (o t) d", p=P)).then_inc(x_in, 16)
                    sp.dma_start(xn[:, CTILES:, :], a["x"].rearrange("o (t p) d -> p (o t) d", p=P)).then_inc(x_in, 16)

                @block.scalar
                def _(act):
                    with nc.allow_non_contiguous_dma(reason="1024 elements"):
                        act.dma_start(cT[:, :, 0], a["c"].rearrange("o (k p) -> p (o k)", p=P)).then_inc(c_in, 16)
                        act.dma_start(cT[:, :, 1], a["c_ctx"].rearrange("(k p) -> p k", p=P)).then_inc(c_in, 16)
                    act.wait_ge(c_in, 32)
                    act.activation(self.sT[:, :, :], cT[:, :, :], ACT.Silu)
                    for k in range(1, KD, 2):
                        act.wait_ge(turned, k + 1)
                        act.activation(self.xT[:, k, :], ps[:, k % 4, LC:], ACT.Copy).then_inc(copied_odd, 1)

                @block.tensor
                def _(pe):
                    pe.wait_ge(consts_in, 16)
                    pe.wait_ge(x_in, 32)
                    for k in range(KD):
                        if k >= 4:
                            pe.wait_ge(copied_odd if k % 2 else copied_even, (k - 4) // 2 + 1)
                        for t in range(TILES):
                            last = pe.transpose(ps[:, k % 4, LC + t * P:LC + (t + 1) * P],
                                                xn[:, t, k * P:(k + 1) * P], self.c("ident"))
                        last.then_inc(turned, 1)

                @block.vector
                def _(dve):
                    for j, v in enumerate((EPS, EPS, P * EPS, 1.0) + tuple(EPS / (0.2 + 0.6 * math.exp(-0.3 * l)) ** 2 for l in range(DEPTH))):
                        dve.memset(self.eps[:, j:j + 1], v)
                    for k in range(0, KD, 2):
                        dve.wait_ge(turned, k + 1)
                        dve.tensor_copy(self.xT[:, k, :], ps[:, k % 4, LC:]).then_inc(copied_even, 1)

    def modulation(self, l):
        nc, a, ps = self.nc, self.a, self.ps
        CH = 512
        NCH = 6 * D // CH
        with Stage(self) as s:
            loaded = s.signals(2)
            small_in, slot_free, multiplied, own, ps_free = s.signals(5)
            w = s.sb("w", [P, 2, KD, CH])
            bT = s.sb("bT", [P, 6 * KD])
            gT = s.sb("gT", [P, 2, KD])
            src = a["w_mod"][l].rearrange("(k p) n -> p k n", p=P)
            with nc.Block() as block:
                @block.sync
                def _(sp):
                    with sp.Fori(0, NCH // 2) as i:
                        for j in range(2):
                            sp.wait_ge(slot_free, i * 2 + (j + 1))
                            sp.dma_start(w[:, j], src[:, :, bass.ts(i * 2 + j, CH)]).then_inc(loaded[j], 16)

                @block.scalar
                def _(act):
                    with nc.allow_non_contiguous_dma(reason="vectors turned to columns"):
                        act.dma_start(bT[:, :], a["b_mod"][l].rearrange("(k p) -> p k", p=P)).then_inc(small_in, 16)
                        act.dma_start(gT[:, 0], a["norm1_g"][l].rearrange("(k p) -> p k", p=P)).then_inc(small_in, 16)
                        act.dma_start(gT[:, 1], a["norm2_g"][l].rearrange("(k p) -> p k", p=P)).then_inc(small_in, 16)
                        for j, name in enumerate(("da_q_norm_g", "da_k_norm_g")):
                            for half in range(2):
                                act.dma_start(self.cols[half * DH:(half + 1) * DH, j:j + 1], a[name][l].rearrange("(p o) -> p o", o=1)).then_inc(small_in, 16)
                        for j, name in enumerate(("da_subln_g", "gdn_out_norm_g")):
                            act.dma_start(self.cols[:, 2 + j:3 + j], a[name][l].rearrange("(p o) -> p o", o=1)).then_inc(small_in, 16)

                @block.tensor
                def _(pe):
                    pe.sem_inc(slot_free, 2)
                    pe.sem_inc(ps_free, 2)
                    with pe.Fori(0, NCH // 2) as i:
                        for j in range(2):
                            pe.wait_ge(loaded[j], i * 16 + 16)
                            pe.wait_ge(ps_free, i * 2 + (j + 1))
                            for b in range(CH // P):
                                for k in range(KD):
                                    last = pe.matmul(ps[:, 2 * j, 2 * b:2 * b + 2], w[:, j, k, b * P:(b + 1) * P],
                                                     self.sT[:, k, :], start=(k == 0), stop=(k == KD - 1))
                            last.then_inc(multiplied, 1)
                            pe.wait_ge(multiplied, i * 2 + (j + 1))
                            pe.sem_inc(slot_free, 1)

                @block.vector
                def _(dve):
                    step = Steps(dve, own)
                    dve.wait_ge(small_in, 9 * 16)
                    nb = CH // P
                    with dve.Fori(0, NCH // 2) as i:
                        for j in range(2):
                            hold(dve, multiplied, i * 2 + (j + 1))
                            dve.tensor_tensor(self.modT[:, bass.ts(i * 2 + j, nb), :],
                                              ps[:, 2 * j, 0:2 * nb].rearrange("p (b s) -> p b s", s=2),
                                              each(bT[:, bass.ts(i * 2 + j, nb)], 2), ALU.add).then_inc(ps_free, 1)
                    dve.wait_ge(ps_free, NCH + 2)
                    for gain, part, which in ((self.gain1, 1, 0), (self.gain2, 4, 1)):
                        step(dve.tensor_scalar(gain[:, :, :], self.modT[:, part * KD:(part + 1) * KD, :], 1.0, None, ALU.add))
                        step.settle()
                        step(dve.tensor_tensor(gain[:, :, :], gain[:, :, :], each(gT[:, which], 2), ALU.mult))

    def norm(self, gain, shift, lo=0):
        nc, ps = self.nc, self.ps
        with Stage(self) as s:
            squared, summed, rooted, inverted, scaled, scaled_used = s.signals(6)
            sq = s.sb("sq", [P, 2, T])
            rs = s.sb("rs", [P, T])
            ri = s.sb("ri", [P, T])
            xr = s.sb("xr", [P, 2, T])
            with nc.Block() as block:
                @block.scalar
                def _(act):
                    for k in range(KD):
                        if k >= 2:
                            act.wait_ge(summed, k - 1)
                        act.activation(sq[:, k % 2, lo:], self.xT[:, k, lo:], ACT.Square).then_inc(squared, 1)
                    act.wait_ge(summed, KD)
                    act.activation(rs[:, lo:], ps[:, 0, LC + lo:], ACT.Sqrt, bias=self.eps[:, 0:1], scale=1.0 / D).then_inc(rooted, 1)
                    for k in range(KD):
                        act.wait_ge(scaled, k + 1)
                        for b, e, kind in KIND_RANGE:
                            if e > lo:
                                last = act.activation(self.hT[:, k, b:e], xr[:, k % 2, b:e], ACT.Identity,
                                                      bias=self.modT[:, shift * KD + k, kind:kind + 1],
                                                      scale=gain[:, k, kind:kind + 1])
                        last.then_inc(scaled_used, 1)

                @block.tensor
                def _(pe):
                    for k in range(KD):
                        pe.wait_ge(squared, k + 1)
                        for b, e in spans(lo):
                            last = pe.matmul(ps[:, 0, LC + b:LC + e], self.c("ones"), sq[:, k % 2, b:e],
                                             start=(k == 0), stop=(k == KD - 1))
                        last.then_inc(summed, 1)

                @block.vector
                def _(dve):
                    dve.wait_ge(rooted, 1)
                    dve.reciprocal(ri[:, lo:], rs[:, lo:]).then_inc(inverted, 1)
                    dve.wait_ge(inverted, 1)
                    for k in range(KD):
                        if k >= 2:
                            dve.wait_ge(scaled_used, k - 1)
                        dve.tensor_tensor(xr[:, k % 2, lo:], self.xT[:, k, lo:], ri[:, lo:], ALU.mult).then_inc(scaled, 1)

    def project(self, s, block, w_view, rhs, nblocks, lo, block_done, ps_free, gates=()):
        loaded = s.signals(2)
        slot_free, = s.signals(1)
        w = s.sb("w", [P, 2, KD, 2 * P])
        trips = nblocks // 4

        @block.sync
        def _(sp):
            with sp.Fori(0, trips) as i:
                for j in range(2):
                    sp.wait_ge(slot_free, i * 2 + (j + 1))
                    sp.dma_start(w[:, j], w_view[:, :, bass.ts(i * 2 + j, 2 * P)]).then_inc(loaded[j], 16)

        @block.tensor
        def _(pe):
            pe.sem_inc(slot_free, 2)
            pe.sem_inc(ps_free, 2)
            with pe.Fori(0, trips) as i:
                for j in range(2):
                    pe.wait_ge(loaded[j], i * 16 + 16)
                    for h in range(2):
                        pe.wait_ge(ps_free, i * 4 + (2 * j + h + 1))
                        for k in range(KD):
                            for b, e in spans(lo):
                                last = pe.matmul(self.ps[:, h, LC + b:LC + e], w[:, j, k, h * P:(h + 1) * P],
                                                 rhs[:, k, b:e], start=(k == 0), stop=(k == KD - 1))
                        last.then_inc(block_done, 1)
                    pe.wait_ge(block_done, i * 4 + (2 * j + 2))
                    pe.sem_inc(slot_free, 1)

    def w_in(self, l, col, n):
        return self.a["w_in"][l].rearrange("(k p) n -> p k n", p=P)[:, :, col:col + n]

    def gdn_qkv(self, l, qkvT):
        nc, ps = self.nc, self.ps
        NB = 12
        with Stage(self) as s:
            block_done, ps_free, padded, conved, own, small_in, silud, zeroed = s.signals(8)
            cb = s.sb("cb", [P, CW])
            cv = s.sb("cv", [P, 5, CW - 4])
            taps = s.sb("taps", [P, NB, 5])
            with nc.Block() as block:
                self.project(s, block, self.w_in(l, C_QKV, NB * P), self.hT, NB, 0, block_done, ps_free)

                @block.scalar
                def _(act):
                    with nc.allow_non_contiguous_dma(reason="7680 taps"):
                        for j in range(5):
                            act.dma_start(taps[:, :, j], self.a["gdn_conv_w"][l, j].rearrange("(b p) -> p b", p=P)).then_inc(small_in, 16)
                    act.wait_ge(zeroed, 1)
                    with act.Fori(0, NB // 2) as i:
                        for j in range(2):
                            act.wait_ge(block_done, i * 2 + (j + 1))
                            act.activation(cb[:, PAD:PAD + LC], ps[:, j, LC:2 * LC], ACT.Copy)
                            act.activation(cb[:, 3 * PAD + LC:3 * PAD + T], ps[:, j, 2 * LC:], ACT.Copy).then_inc(padded, 1)
                            hold(act, conved, i * 2 + (j + 1))
                            act.activation(qkvT[:, i * 2 + j, 0:LC], cv[:, 4, 0:LC], ACT.Silu)
                            act.activation(qkvT[:, i * 2 + j, LC:], cv[:, 4, LC + 2 * PAD:], ACT.Silu).then_inc(silud, 1)

                @block.vector
                def _(dve):
                    step = Steps(dve, own)
                    dve.memset(cb[:, :], 0.0).then_inc(zeroed, 1)
                    dve.wait_ge(small_in, 5 * 16)
                    n = CW - 4
                    with dve.Fori(0, NB // 2) as i:
                        step.loop(i, 8)
                        for j in range(2):
                            hold(dve, padded, i * 2 + (j + 1))
                            dve.sem_inc(ps_free, 1)
                            dve.tensor_scalar(cv[:, 0], cb[:, 0:n], taps[:, i * 2 + j, 0:1], None, ALU.mult).then_inc(own, 1)
                            step.n += 1
                            for tap in range(1, 5):
                                step.settle()
                                ins = dve.scalar_tensor_tensor(cv[:, tap], cb[:, tap:tap + n], taps[:, i * 2 + j, tap:tap + 1],
                                                               cv[:, tap - 1], ALU.mult, ALU.add)
                                if tap < 4:
                                    step(ins)
                                else:
                                    ins.then_inc(conved, 1)
                        step.end(NB // 2)

    def head_norm(self, src, ones, nblocks, lo, root, finish):
        nc, ps = self.nc, self.ps
        with Stage(self) as s:
            squared, summed, rooted, own, done = s.signals(5)
            sq = s.sb("sq", [P, 2, T])
            rs = s.sb("rs", [P, 2, T])
            ri = s.sb("ri", [P, 2, T])
            with nc.Block() as block:
                @block.scalar
                def _(act):
                    for b in range(nblocks + 1):
                        if b < nblocks:
                            if b >= 2:
                                act.wait_ge(summed, b - 1)
                            act.activation(sq[:, b % 2, lo:], src[:, b, lo:], ACT.Square).then_inc(squared, 1)
                        if b:
                            act.wait_ge(summed, b)
                            if b >= 3:
                                act.wait_ge(done, b - 2)
                            scale, eps = root(b - 1)
                            act.activation(rs[:, (b - 1) % 2, lo:], ps[:, (b - 1) % 2, LC + lo:], ACT.Sqrt,
                                           scale=scale, bias=eps).then_inc(rooted, 1)

                @block.tensor
                def _(pe):
                    for b in range(nblocks):
                        pe.wait_ge(squared, b + 1)
                        if b >= 2:
                            pe.wait_ge(rooted, b - 1)
                        for first, end in spans(lo):
                            last = pe.matmul(ps[:, b % 2, LC + first:LC + end], self.c(ones), sq[:, b % 2, first:end], start=True, stop=True)
                        last.then_inc(summed, 1)

                @block.vector
                def _(dve):
                    step = Steps(dve, own)
                    for b in range(nblocks):
                        dve.wait_ge(rooted, b + 1)
                        step(dve.reciprocal(ri[:, b % 2, lo:], rs[:, b % 2, lo:]))
                        step.settle()
                        finish(dve, step, b, ri[:, b % 2]).then_inc(done, 1)

    def gdn_unit(self, qkvT):
        def root(b):
            return (float(P), self.eps[:, 2:3]) if b < HEADS else (1.0, self.eps[:, 0:1])

        def finish(dve, step, b, r):
            return dve.tensor_tensor(qkvT[:, b, :], qkvT[:, b, :], r, ALU.mult)

        self.head_norm(qkvT, "ones", 2 * HEADS, 0, root, finish)

    def gdn_gates(self, l, betaT, gcT, beta_nat, gc_nat, kscale):
        nc, ps = self.nc, self.ps
        with Stage(self) as s:
            small_in, made, own, own_act, turned, flat, summed = s.signals(7)
            w = s.sb("w", [P, KD, 16])
            cols = s.sb("cols", [8, 4])
            gx = s.sb("gx", [8, T])
            ga = s.sb("ga", [8, T])
            ge = s.sb("ge", [8, T])
            gl = s.sb("gl", [8, T])
            gm = s.sb("gm", [8, T])
            gT = s.sb("gT", [8, T])
            gn = s.sb("gn", [P, 2, TILES, HEADS])
            eg = s.sb("eg", [P, TILES, 8])
            with nc.Block() as block:
                @block.sync
                def _(sp):
                    with nc.allow_non_contiguous_dma(reason="16 columns, 16 numbers"):
                        sp.dma_start(w[:, :, :], self.w_in(l, C_BA, 16)).then_inc(small_in, 16)
                        sp.dma_start(cols[:, 0:1], self.a["gdn_dt_bias"][l].rearrange("d (h o) -> (d h) o", o=1)).then_inc(small_in, 16)
                        sp.dma_start(cols[:, 1:2], self.a["gdn_a_log"][l].rearrange("d (h o) -> (d h) o", o=1)).then_inc(small_in, 16)

                @block.tensor
                def _(pe):
                    pe.wait_ge(small_in, 48)
                    for half in range(2):
                        for k in range(KD):
                            for lo, hi in spans(0):
                                last = pe.matmul(ps[0:8, half, LC + lo:LC + hi], w[:, k, 8 * half:8 * half + 8],
                                                 self.hT[:, k, lo:hi], start=(k == 0), stop=(k == KD - 1))
                    last.then_inc(made, 1)
                    pe.wait_ge(flat, 1)
                    for t in range(TILES):
                        pe.transpose(ps[:, 2, 8 * t:8 * t + 8], betaT[:, t * P:(t + 1) * P], self.c("ident")[0:8, 0:8])
                        last = pe.transpose(ps[:, 2, 512 + 8 * t:512 + 8 * t + 8], gT[:, t * P:(t + 1) * P], self.c("ident")[0:8, 0:8])
                    last.then_inc(turned, 1)
                    pe.wait_ge(summed, 1)
                    for d, tri in enumerate(("upper", "lower")):
                        pe.matmul(ps[:, 3, d * 64:d * 64 + TILES * HEADS], self.c(tri), gn[:, d].rearrange("p t h -> p (t h)"), start=True, stop=True)
                        for t in range(TILES):
                            last = pe.matmul(ps[0:HEADS, d, LC + t * P:LC + (t + 1) * P], gn[:, d, t, :], self.c(tri), start=True, stop=True)
                    last.then_inc(turned, 1)

                @block.scalar
                def _(act):
                    step = Steps(act, own_act)
                    act.wait_ge(small_in, 48)
                    step(act.activation(cols[:, 2:3], cols[:, 1:2], ACT.Exp))
                    act.wait_ge(made, 1)
                    step(act.activation(betaT[:, :], ps[0:8, 0, LC:], ACT.Sigmoid))
                    act.wait_ge(own, 1)
                    step(act.activation(ga[:, :], gx[:, :], ACT.Abs))
                    step.settle()
                    step(act.activation(ge[:, :], ga[:, :], ACT.Exp, scale=-1.0))
                    step.settle()
                    step(act.activation(gl[:, :], ge[:, :], ACT.Ln, bias=self.eps[0:8, 3:4]))
                    act.wait_ge(own, 7)
                    step(act.activation(eg[:, :, :], gc_nat[:, :, :], ACT.Exp))

                @block.vector
                def _(dve):
                    step = Steps(dve, own)
                    dve.wait_ge(made, 1)
                    step(dve.tensor_scalar(gx[:, :], ps[0:8, 1, LC:], cols[:, 0:1], None, ALU.add))
                    dve.wait_ge(own_act, 5)
                    step.settle()
                    step(dve.scalar_tensor_tensor(gm[:, :], gx[:, :], 0.0, gl[:, :], ALU.max, ALU.add))
                    step.settle()
                    dve.tensor_scalar(gT[:, :], gm[:, :], cols[:, 2:3], -1.0, ALU.mult, ALU.mult).then_inc(flat, 1)
                    dve.wait_ge(turned, 1)
                    step(dve.tensor_copy(beta_nat[:, :, :], ps[:, 2, 0:8 * TILES].rearrange("p (t c) -> p t c", c=8)))
                    for d in range(2):
                        last = dve.tensor_copy(gn[:, d], ps[:, 2, 512:512 + 8 * TILES].rearrange("p (t c) -> p t c", c=8)[:, :, HEADS * d:HEADS * (d + 1)])
                    last.then_inc(summed, 1)
                    dve.wait_ge(turned, 2)
                    for d in range(2):
                        step(dve.tensor_copy(gcT[d][:, :], ps[0:HEADS, d, LC:]))
                    for d in range(2):
                        step(dve.tensor_copy(gc_nat[:, :, HEADS * d:HEADS * (d + 1)],
                                             ps[:, 3, d * 64:d * 64 + TILES * HEADS].rearrange("p (t h) -> p t h", h=HEADS)))
                    dve.wait_ge(own_act, 6)
                    dve.tensor_tensor(kscale[:, :, :], eg[:, :, :], beta_nat[:, :, :], ALU.mult)

    def gdn_scan(self, qkvT, oaT, betaT, gcT, beta_nat, gc_nat, kscale):
        nc, ps = self.nc, self.ps
        H4 = HEADS * P
        top = LEVELS - 1
        V_LAST = 6 + 2 * top
        T_LAST = 3 + 2 * top + 4
        A_LAST = 4
        with Stage(self) as s:
            t_done, v_done, a_done = s.signals(2), s.signals(2), s.signals(2)
            own, zeroed = s.signals(2)
            names = ("kT", "vT", "kb", "diff", "dec", "eg", "qd", "kd", "ke", "vb", "low", "qk", "W", "Wt", "X", "wT", "vn", "state")
            bufs = [{n: s.sb(f"{n}{d}", [P, H4]) for n in names} for d in range(2)]
            kds = [s.sb(f"kds{d}", [P, HEADS]) for d in range(2)]
            kde = [s.sb(f"kde{d}", [P, HEADS]) for d in range(2)]

            def bank(d, n):
                return ps[:, 2 * d + n // 2, 512 * (n % 2):512 * (n % 2) + H4]

            def heads(ap):
                return ap.rearrange("p (h c) -> p h c", h=HEADS)

            def hd(ap, h):
                return ap[:, h * P:(h + 1) * P]

            def mask(d, lv):
                return over(self.c("masks")[:, (d * LEVELS + lv) * P:(d * LEVELS + lv + 1) * P], HEADS)

            loops = ((0, CTILES, CTILES - 1), (CTILES, TILES, CTILES + TILES - 1))

            def tile(d, i, mirror):
                return i if d == 0 else (i * -1) + mirror

            with nc.Block() as block:
                @block.tensor
                def _(pe):
                    def four(out, lhs, rhs, start=True, stop=True):
                        for h in range(HEADS):
                            last = pe.matmul(hd(out, h), hd(lhs, h), hd(rhs, h), start=start, stop=stop)
                        return last

                    pe.wait_ge(zeroed, 1)
                    for first, end, mirror in loops:
                        with pe.Fori(first, end) as i:
                            for d, b in enumerate(bufs):
                                tok = bass.ts(tile(d, i, mirror), P)
                                pe.wait_ge(v_done[d], i * V_LAST + 1)
                                for h in range(HEADS):
                                    pe.transpose(hd(bank(d, 2), h), hd(b["kT"][:, :], h), self.c("ident"))
                                    pe.transpose(hd(bank(d, 3), h), hd(b["vT"][:, :], h), self.c("ident"))
                                for h in range(HEADS):
                                    j = HEADS * d + h
                                    pe.matmul(hd(bank(d, 1), h), self.c("sel")[0:8, j * P:(j + 1) * P], betaT[:, tok], start=True, stop=True)
                                    last = pe.matmul(hd(bank(d, 0), h), self.c("sel")[0:HEADS, h * P:(h + 1) * P], gcT[d][:, tok], start=True, stop=True)
                                last.then_inc(t_done[d], 1)
                            for d, b in enumerate(bufs):
                                tok = bass.ts(tile(d, i, mirror), P)
                                pe.wait_ge(v_done[d], i * V_LAST + 3)
                                four(bank(d, 0), b["kT"][:, :], b["kb"][:, :])
                                for h in range(HEADS):
                                    last = pe.matmul(hd(bank(d, 1), h), hd(b["kT"][:, :], h), qkvT[:, h, tok], start=True, stop=True)
                                last.then_inc(t_done[d], 1)
                            for d, b in enumerate(bufs):
                                pe.wait_ge(v_done[d], i * V_LAST + 4)
                                four(bank(d, 2), b["low"][:, :], self.c("ident4")).then_inc(t_done[d], 1)
                            for lv in range(1, LEVELS):
                                for d, b in enumerate(bufs):
                                    pe.wait_ge(v_done[d], i * V_LAST + 3 + 2 * lv)
                                    four(bank(d, 2), b["low"][:, :], b["W"][:, :]).then_inc(t_done[d], 1)
                                for d, b in enumerate(bufs):
                                    pe.wait_ge(v_done[d], i * V_LAST + 4 + 2 * lv)
                                    if lv < top:
                                        four(bank(d, 3), b["Wt"][:, :], b["X"][:, :])
                                    four(bank(d, 0), b["X"][:, :], b["Wt"][:, :]).then_inc(t_done[d], 1)
                            for d, b in enumerate(bufs):
                                pe.wait_ge(v_done[d], i * V_LAST + 5 + 2 * top)
                                four(bank(d, 1), b["ke"][:, :], b["Wt"][:, :]).then_inc(t_done[d], 1)
                            for d, b in enumerate(bufs):
                                pe.wait_ge(a_done[d], i * A_LAST + 3)
                                for h in range(HEADS):
                                    pe.matmul(hd(bank(d, 2), h), hd(b["Wt"][:, :], h), hd(b["vb"][:, :], h), start=True, stop=False)
                                    last = pe.matmul(hd(bank(d, 2), h), hd(b["wT"][:, :], h), hd(b["state"][:, :], h), start=False, stop=True)
                                last.then_inc(t_done[d], 1)
                            for d, b in enumerate(bufs):
                                pe.wait_ge(a_done[d], i * A_LAST + 4)
                                for h in range(HEADS):
                                    pe.matmul(hd(bank(d, 3), h), hd(b["state"][:, :], h), hd(b["qd"][:, :], h), start=True, stop=False)
                                    last = pe.matmul(hd(bank(d, 3), h), hd(b["vn"][:, :], h), hd(b["qk"][:, :], h), start=False, stop=True)
                                last.then_inc(t_done[d], 1)
                                four(bank(d, 0), b["kd"][:, :], b["vn"][:, :]).then_inc(t_done[d], 1)

                @block.scalar
                def _(act):
                    for first, end, mirror in loops:
                        with act.Fori(first, end) as i:
                            for d, b in enumerate(bufs):
                                act.wait_ge(t_done[d], i * T_LAST + 1)
                                act.activation(b["eg"][:, :], bank(d, 0), ACT.Exp).then_inc(a_done[d], 1)
                                act.wait_ge(v_done[d], i * V_LAST + 2)
                                act.activation(b["dec"][:, :], b["diff"][:, :], ACT.Exp)
                                act.activation(kde[d][:, :], kds[d][:, :], ACT.Exp).then_inc(a_done[d], 1)
                            for d, b in enumerate(bufs):
                                act.wait_ge(t_done[d], i * T_LAST + T_LAST - 3)
                                act.activation(b["wT"][:, :], bank(d, 1), ACT.Copy, scale=-1.0).then_inc(a_done[d], 1)
                            for d, b in enumerate(bufs):
                                act.wait_ge(t_done[d], i * T_LAST + T_LAST - 2)
                                act.activation(b["vn"][:, :], bank(d, 2), ACT.Copy).then_inc(a_done[d], 1)

                @block.vector
                def _(dve):
                    step = Steps(dve, own)
                    for d, b in enumerate(bufs):
                        step(dve.memset(b["state"][:, :], 0.0))
                    step(dve.memset(oaT[:, :, :], 0.0))
                    step.settle()
                    dve.sem_inc(zeroed, 1)
                    for first, end, mirror in loops:
                        with dve.Fori(first, end) as i:
                            step.loop((i - first) if first else i, 46)
                            for d, b in enumerate(bufs):
                                tok = bass.ts(tile(d, i, mirror), P)
                                step(dve.tensor_copy(heads(b["kT"][:, :]), qkvT[:, HEADS:2 * HEADS, tok]))
                                dve.tensor_copy(heads(b["vT"][:, :]), qkvT[:, 2 * HEADS:3 * HEADS, tok]).then_inc(v_done[d], 1)
                            for d, b in enumerate(bufs):
                                t = tile(d, i, mirror)
                                lastcol = P - 1 if d == 0 else 0
                                hold(dve, t_done[d], i * T_LAST + 1)
                                hold(dve, a_done[d], i * A_LAST + 1)
                                for h in range(HEADS):
                                    step(dve.tensor_scalar(hd(b["diff"][:, :], h), hd(bank(d, 0), h), gc_nat[:, t, HEADS * d + h:HEADS * d + h + 1],
                                                           0.0, ALU.subtract, ALU.min))
                                dve.tensor_tensor(kds[d][:, :], heads(bank(d, 0))[:, :, lastcol], gc_nat[:, t, HEADS * d:HEADS * (d + 1)],
                                                  ALU.subtract).then_inc(v_done[d], 1)
                                dve.tensor_tensor(b["kb"][:, :], b["kT"][:, :], bank(d, 1), ALU.mult).then_inc(v_done[d], 1)
                            for d, b in enumerate(bufs):
                                t = tile(d, i, mirror)
                                mine = slice(HEADS * d, HEADS * (d + 1))
                                hold(dve, a_done[d], i * A_LAST + 2)
                                step(dve.tensor_tensor(heads(b["dec"][:, :]), heads(b["dec"][:, :]), over(self.c("lower" if d else "upper"), HEADS), ALU.mult))
                                step(dve.tensor_tensor(heads(b["qd"][:, :]), qkvT[:, 0:HEADS, bass.ts(t, P)], heads(b["eg"][:, :]), ALU.mult))
                                step(dve.tensor_tensor(heads(b["kd"][:, :]), heads(bank(d, 2)), each(kde[d][:, :], P), ALU.mult))
                                step(dve.tensor_tensor(heads(b["ke"][:, :]), heads(bank(d, 2)), each(kscale[:, t, mine], P), ALU.mult))
                                step(dve.tensor_tensor(heads(b["vb"][:, :]), heads(bank(d, 3)), each(beta_nat[:, t, mine], P), ALU.mult))
                            for d, b in enumerate(bufs):
                                step.settle(back=5 * (1 - d))
                                hold(dve, t_done[d], i * T_LAST + 2)
                                step(dve.tensor_tensor(b["low"][:, :], bank(d, 0), b["dec"][:, :], ALU.mult))
                                step(dve.tensor_tensor(b["qk"][:, :], bank(d, 1), b["dec"][:, :], ALU.mult))
                                step.settle(back=1)
                                step(dve.tensor_tensor(heads(b["X"][:, :]), heads(b["low"][:, :]), mask(1 - d, 0), ALU.mult))
                                step.settle()
                                dve.tensor_tensor(b["Wt"][:, :], self.c("ident4"), b["X"][:, :], ALU.subtract).then_inc(v_done[d], 1)
                            for d, b in enumerate(bufs):
                                hold(dve, t_done[d], i * T_LAST + 3)
                                step(dve.tensor_tensor(heads(b["X"][:, :]), heads(bank(d, 2)), mask(d, 0), ALU.mult))
                                step.settle()
                                dve.tensor_tensor(b["W"][:, :], self.c("ident4"), b["X"][:, :], ALU.subtract).then_inc(v_done[d], 1)
                            for lv in range(1, LEVELS):
                                for d, b in enumerate(bufs):
                                    dve.wait_ge(t_done[d], i * T_LAST + 2 + 2 * lv)
                                    dve.tensor_tensor(heads(b["X"][:, :]), heads(bank(d, 2)), mask(d, lv), ALU.mult).then_inc(v_done[d], 1)
                                for d, b in enumerate(bufs):
                                    dve.wait_ge(t_done[d], i * T_LAST + 3 + 2 * lv)
                                    if lv < top:
                                        step(dve.tensor_tensor(b["W"][:, :], b["W"][:, :], bank(d, 3), ALU.subtract))
                                    dve.tensor_tensor(b["Wt"][:, :], b["Wt"][:, :], bank(d, 0), ALU.subtract).then_inc(v_done[d], 1)
                            for d, b in enumerate(bufs):
                                tok = bass.ts(tile(d, i, mirror), P)
                                lastcol = P - 1 if d == 0 else 0
                                hold(dve, t_done[d], i * T_LAST + T_LAST)
                                step(dve.tensor_tensor(oaT[:, :, tok], oaT[:, :, tok], heads(bank(d, 3)), ALU.add))
                                for h in range(HEADS):
                                    last = dve.scalar_tensor_tensor(hd(b["state"][:, :], h), hd(b["state"][:, :], h), hd(b["eg"][:, :], h)[:, lastcol:lastcol + 1],
                                                                    hd(bank(d, 0), h), ALU.mult, ALU.add)
                                    if h < HEADS - 1:
                                        step(last)
                                last.then_inc(v_done[d], 1)
                            step.end(end - first)

    def columns(self, l, parts, lo):
        nc, ps = self.nc, self.ps
        NB = 4
        with Stage(self) as s:
            loaded = s.signals(2)
            slot_free, block_done, ps_free = s.signals(3)
            w = s.sb("w", [P, 2, KD, 2 * P])
            with nc.Block() as block:
                @block.sync
                def _(sp):
                    for n, (col, func, dst, first) in enumerate(parts):
                        for j in range(2):
                            if n:
                                sp.wait_ge(slot_free, 2 * n + j - 1)
                            sp.dma_start(w[:, j], self.w_in(l, col + 2 * P * j, 2 * P)).then_inc(loaded[j], 16)

                @block.tensor
                def _(pe):
                    for n, (col, func, dst, first) in enumerate(parts):
                        for b in range(NB):
                            m = NB * n + b
                            pe.wait_ge(loaded[b // 2], 16 * (n + 1))
                            if m >= 4:
                                pe.wait_ge(ps_free, m - 3)
                            for k in range(KD):
                                for lo_, hi in spans(first):
                                    last = pe.matmul(ps[:, m % 4, LC + lo_:LC + hi], w[:, b // 2, k, (b % 2) * P:(b % 2 + 1) * P],
                                                     self.hT[:, k, lo_:hi], start=(k == 0), stop=(k == KD - 1))
                            last.then_inc(block_done, 1)
                            if b % 2:
                                pe.wait_ge(block_done, m + 1)
                                pe.sem_inc(slot_free, 1)

                @block.scalar
                def _(act):
                    for n, (col, func, dst, first) in enumerate(parts):
                        for b in range(NB):
                            m = NB * n + b
                            act.wait_ge(block_done, m + 1)
                            act.activation(dst[:, b, first:], ps[:, m % 4, LC + first:], func).then_inc(ps_free, 1)

    def values(self, l, vda, vhat, lo):
        nc, ps = self.nc, self.ps
        W = HEADS * P
        with Stage(self) as s:
            w_in, g_in, made, taken, squared, rooted, own = s.signals(7)
            w = s.sb("w", [P, 2, KD, W])
            gb = s.sb("gb", [P, W])
            vg = s.sb("vg", [P, 2, W])
            junk = s.sb("junk", [P, 2, W])
            ss = s.sb("ss", [P, TILES])
            root = s.sb("root", [P, TILES])
            inv = s.sb("inv", [P, TILES])
            first = lo // P
            with nc.Block() as block:
                @block.sync
                def _(sp):
                    sp.dma_start(w[:, 0], self.w_in(l, C_DV, W)).then_inc(w_in, 16)
                    sp.dma_start(w[:, 1], self.w_in(l, C_V, W)).then_inc(w_in, 16)
                    sp.dma_start(gb[:, :], self.a["cmlp_v_norm_g"][l].partition_broadcast(P)).then_inc(g_in, 16)

                @block.tensor
                def _(pe):
                    pe.wait_ge(w_in, 32)
                    n = 0
                    for which in range(2):
                        for t in range(first if which else 0, TILES):
                            if n >= 4:
                                pe.wait_ge(taken, n - 3)
                            for k in range(KD):
                                last = pe.matmul(ps[:, n % 4, 0:W], self.hT[:, k, t * P:(t + 1) * P], w[:, which, k, :],
                                                 start=(k == 0), stop=(k == KD - 1))
                            last.then_inc(made, 1)
                            n += 1

                @block.scalar
                def _(act):
                    for t in range(TILES):
                        act.wait_ge(made, t + 1)
                        act.activation(vda[:, t, :], ps[:, t % 4, 0:W], ACT.Copy).then_inc(taken, 1)
                    for t in range(first, TILES):
                        n = TILES + t - first
                        act.wait_ge(made, n + 1)
                        act.activation(vhat[:, t, :], ps[:, n % 4, 0:W], ACT.Gelu_apprx_tanh).then_inc(taken, 1)
                    act.wait_ge(squared, TILES - first)
                    act.activation(root[:, first:], ss[:, first:], ACT.Sqrt, scale=1.0 / W, bias=self.eps[:, 0:1]).then_inc(rooted, 1)

                @block.vector
                def _(dve):
                    for t in range(first, TILES):
                        dve.wait_ge(taken, TILES + t - first + 1)
                        if t - first >= 2:
                            dve.wait_ge(squared, t - first - 1)
                        dve.tensor_tensor_reduce(out=junk[:, t % 2], in0=vhat[:, t, :], in1=vhat[:, t, :], scale=1.0, scalar=0.0,
                                                 op0=ALU.mult, op1=ALU.add, accum_out=ss[:, t:t + 1]).then_inc(squared, 1)
                    dve.wait_ge(rooted, 1)
                    dve.wait_ge(g_in, 16)
                    dve.reciprocal(inv[:, first:], root[:, first:]).then_inc(own, 1)
                    dve.wait_ge(own, 1)
                    for t in range(first, TILES):
                        dve.scalar_tensor_tensor(vhat[:, t, :], vhat[:, t, :], inv[:, t:t + 1], gb[:, :], ALU.mult, ALU.mult)

    def chunk_mlp(self, l, ybT, vhat, lo):
        nc, ps = self.nc, self.ps
        W = HEADS * P
        first = lo // P
        with Stage(self) as s:
            in_, turned, flat, mixed, own, done = s.signals(6)
            ws = s.sb("ws", [P, HEADS, P])
            wsT = s.sb("wsT", [P, W])
            bs = s.sb("bs", [P, W])
            sv = s.sb("sv", [P, 2, W])
            with nc.Block() as block:
                @block.sync
                def _(sp):
                    sp.dma_start(ws[:, :, :], self.a["cmlp_w_s"][l].rearrange("g p q -> p g q")).then_inc(in_, 16)
                    sp.dma_start(bs[:, :], self.a["cmlp_b_s"][l].rearrange("g p -> (g p)").partition_broadcast(P)).then_inc(in_, 16)

                @block.tensor
                def _(pe):
                    pe.wait_ge(in_, 32)
                    for g in range(HEADS):
                        last = pe.transpose(ps[:, 3, g * P:(g + 1) * P], ws[:, g, :], self.c("ident"))
                    last.then_inc(turned, 1)
                    pe.wait_ge(flat, 1)
                    for t in range(first, TILES):
                        n = t - first
                        if n >= 2:
                            pe.wait_ge(done, n - 1)
                        for g in range(HEADS):
                            last = pe.matmul(ps[:, n % 2, g * P:(g + 1) * P], vhat[:, t, g * P:(g + 1) * P], wsT[:, g * P:(g + 1) * P], start=True, stop=True)
                        last.then_inc(mixed, 1)

                @block.vector
                def _(dve):
                    dve.wait_ge(turned, 1)
                    dve.tensor_copy(wsT[:, :], ps[:, 3, 0:W]).then_inc(flat, 1)
                    for t in range(first, TILES):
                        n = t - first
                        dve.wait_ge(mixed, n + 1)
                        dve.tensor_tensor(sv[:, n % 2], ps[:, n % 2, 0:W], bs[:, :], ALU.add).then_inc(own, 1)
                        dve.wait_ge(own, n + 1)
                        part = ybT[:, :, t * P:(t + 1) * P]
                        dve.tensor_tensor(part, part, sv[:, n % 2].rearrange("p (g c) -> p g c", g=HEADS), ALU.mult).then_inc(done, 1)

    def rotate(self, l, lam_init, qT, kT, lam):
        nc, ps = self.nc, self.ps
        with Stage(self) as s:
            swapped, own, done, lam_in, summed, spread, exps = s.signals(7)
            rot = s.sb("rot", [P, 2, LX])
            cosd = s.sb("cosd", [P, 2, LX])
            row = s.sb("row", [1, 4, DH])
            prod = s.sb("prod", [1, 2, DH])
            sums = s.sb("sums", [1, 2])
            el = s.sb("el", [P, 2])
            blocks = [(qT, h) for h in range(HEADS)] + [(kT, h) for h in range(HEADS)]
            with nc.Block() as block:
                @block.sync
                def _(sp):
                    sp.dma_start(row[:, :, :], self.a["da_lambda"][l:l + 1]).then_inc(lam_in, 16)

                @block.tensor
                def _(pe):
                    for n, (m, h) in enumerate(blocks):
                        if n >= 2:
                            pe.wait_ge(done, n - 1)
                        pe.matmul(ps[:, n % 2, 0:LX], self.c("perm"), m[:, h, LC:], start=True, stop=True).then_inc(swapped, 1)
                    pe.wait_ge(summed, 2)
                    pe.matmul(ps[:, 3, 0:2], self.c("ones")[0:1, :], sums[:, :], start=True, stop=True).then_inc(spread, 1)

                @block.scalar
                def _(act):
                    act.wait_ge(spread, 1)
                    act.activation(el[:, :], ps[:, 3, 0:2], ACT.Exp).then_inc(exps, 1)

                @block.vector
                def _(dve):
                    step = Steps(dve, own)
                    dve.wait_ge(lam_in, 16)
                    dve.tensor_tensor(prod[:, :, :], row[:, 0:4:2, :], row[:, 1:4:2, :], ALU.mult).then_inc(summed, 1)
                    dve.wait_ge(summed, 1)
                    dve.reduce_sum(sums[:, :], prod[:, :, :], axis=AX).then_inc(summed, 1)
                    for n, (m, h) in enumerate(blocks):
                        dve.wait_ge(swapped, n + 1)
                        step(dve.tensor_tensor(rot[:, n % 2], ps[:, n % 2, 0:LX], self.c("sin"), ALU.mult))
                        step(dve.tensor_tensor(cosd[:, n % 2], m[:, h, LC:], self.c("cos"), ALU.mult))
                        step.settle()
                        dve.tensor_tensor(m[:, h, LC:], cosd[:, n % 2], rot[:, n % 2], ALU.add).then_inc(done, 1)
                    dve.wait_ge(exps, 1)
                    dve.tensor_scalar(lam[:, :], el[:, 1:2], el[:, 0:1], -lam_init, ALU.subtract, ALU.add)

    def attend(self, qT, kT, vda, lam, oT, lo):
        nc, ps = self.nc, self.ps
        tiles = list(range(lo // P, TILES))
        NU = len(tiles)
        assert NU % 2 == 0
        SCALE = DH ** -0.5
        with Stage(self) as s:
            copied, scored, maxed, exped, mixed, turned, flat, valued, own, head_free = s.signals(10)
            qh = s.sb("qh", [P, T])
            kh = s.sb("kh", [P, T])
            vh = s.sb("vh", [P, TILES, P])
            p = s.sb("p", [P, 2, 2, T])
            a = s.sb("a", [P, 2, T])
            aT = s.sb("aT", [P, 2, T])
            mx = s.sb("mx", [P, 2, 2])
            nm = s.sb("nm", [P, 2, 2])
            sm = s.sb("sm", [P, 2, 2])
            r = s.sb("r", [P, 2, 2])
            rl = s.sb("rl", [P, 2])

            def keys(u):
                return LC if tiles[u] < CTILES else T

            def out(u):
                return ps[:, 3, 512 * (u % 2):512 * (u % 2) + P]

            with nc.Block() as block:
                @block.tensor
                def _(pe):
                    pe.sem_inc(head_free, 1)
                    with pe.Fori(0, HEADS) as i:
                        def at(n):
                            return i * NU + n

                        def scores(u):
                            for m in range(2):
                                part = slice(DH * m, DH * (m + 1))
                                for b, e in spans(0)[:1 if keys(u) == LC else 2]:
                                    last = pe.matmul(ps[:, m, LC + b:LC + e], qh[part, tiles[u] * P:(tiles[u] + 1) * P], kh[part, b:e], start=True, stop=True)
                            last.then_inc(scored, 1)

                        pe.wait_ge(copied, i * 2 + 2)
                        scores(0)
                        for u in range(NU):
                            pe.wait_ge(exped, at(u + 1))
                            if u + 1 < NU:
                                scores(u + 1)
                            pe.wait_ge(mixed, at(u + 1))
                            nk = keys(u) // P
                            for t in range(nk):
                                last = pe.transpose(ps[:, 2, LC + t * P:LC + (t + 1) * P], a[:, u % 2, t * P:(t + 1) * P], self.c("ident"))
                            last.then_inc(turned, 1)
                            pe.wait_ge(flat, at(u + 1))
                            for t in range(nk):
                                last = pe.matmul(out(u), vh[:, t, :], aT[:, u % 2, t * P:(t + 1) * P], start=(t == 0), stop=(t == nk - 1))
                            last.then_inc(valued, 1)
                        pe.wait_ge(valued, at(NU))
                        pe.sem_inc(head_free, 1)

                @block.scalar
                def _(act):
                    with act.Fori(0, HEADS) as i:
                        def at(n):
                            return i * NU + n

                        def store(u):
                            hold(act, valued, at(u + 1))
                            act.activation(oT[:, i, tiles[u] * P:(tiles[u] + 1) * P], out(u), ACT.Copy)

                        def flatten(u):
                            act.wait_ge(turned, at(u + 1))
                            act.activation(aT[:, u % 2, 0:keys(u)], ps[:, 2, LC:LC + keys(u)], ACT.Copy).then_inc(flat, 1)

                        act.activation(qh[:, lo:], qT[:, i, lo:], ACT.Copy).then_inc(copied, 1)
                        for u in range(NU):
                            act.wait_ge(maxed, at(u + 1))
                            for m in range(2):
                                last = act.activation(p[:, u % 2, m, 0:keys(u)], ps[:, m, LC:LC + keys(u)], ACT.Exp, scale=SCALE,
                                                      bias=nm[:, u % 2, m:m + 1], accum_out=sm[:, u % 2, m:m + 1])
                            last.then_inc(exped, 1)
                            if u >= 2:
                                store(u - 2)
                            if u >= 1:
                                flatten(u - 1)
                        store(NU - 2)
                        flatten(NU - 1)
                        store(NU - 1)

                @block.vector
                def _(dve):
                    step = Steps(dve, own)
                    with dve.Fori(0, HEADS) as i:
                        step.loop(i, 5 * NU + 1)

                        def at(n):
                            return i * NU + n

                        hold(dve, head_free, i + 1)
                        step(dve.tensor_copy(kh[:, :], kT[:, i, :]))
                        dve.tensor_copy(vh[:, :, :], vda[:, :, bass.ts(i, P)]).then_inc(copied, 1)
                        for u in range(NU):
                            w = u % 2
                            hold(dve, scored, at(u + 1))
                            for m in range(2):
                                step(dve.reduce_max(mx[:, w, m:m + 1], ps[:, m, LC:LC + keys(u)], axis=AX))
                            step.settle()
                            dve.tensor_scalar(nm[:, w], mx[:, w], -SCALE, None, ALU.mult).then_inc(maxed, 1)
                            dve.wait_ge(exped, at(u + 1))
                            step(dve.reciprocal(r[:, w], sm[:, w]))
                            step.settle()
                            step(dve.tensor_scalar(rl[:, w:w + 1], r[:, w, 1:2], lam[:, 0:1], None, ALU.mult))
                            step(dve.tensor_scalar(p[:, w, 0, 0:keys(u)], p[:, w, 0, 0:keys(u)], r[:, w, 0:1], None, ALU.mult))
                            step.settle()
                            dve.scalar_tensor_tensor(a[:, w, 0:keys(u)], p[:, w, 1, 0:keys(u)], rl[:, w:w + 1], p[:, w, 0, 0:keys(u)],
                                                     ALU.mult, ALU.add).then_inc(mixed, 1)
                        step.end(HEADS)

    def merge(self, l, yaT, ybT, ycT, yT, lo):
        nc, ps = self.nc, self.ps
        HB = HEADS
        branches = (("w_branch_a", yaT), ("w_branch_b", ybT), ("w_branch_c", ycT))
        with Stage(self) as s:
            loaded = s.signals(2)
            slot_free, multiplied, opened, taken, own = s.signals(5)
            wg = s.sb("wg", [P, 2, 3, KD, P])
            wb = s.sb("wb", [P, 2, 3, HB, P])
            sg = s.sb("sg", [P, 2, T])
            part = s.sb("part", [P, 3, T])
            acc = s.sb("acc", [P, T])
            with nc.Block() as block:
                @block.sync
                def _(sp):
                    with sp.Fori(0, KD // 2) as i:
                        for j in range(2):
                            sp.wait_ge(slot_free, i * 2 + (j + 1))
                            for g, (name, _) in enumerate(branches):
                                sp.dma_start(wg[:, j, g], self.w_in(l, C_G + g * D, D)[:, :, bass.ts(i * 2 + j, P)]).then_inc(loaded[j], 16)
                                sp.dma_start(wb[:, j, g], self.a[name][l].rearrange("(k p) n -> p k n", p=P)[:, :, bass.ts(i * 2 + j, P)]).then_inc(loaded[j], 16)

                @block.tensor
                def _(pe):
                    pe.sem_inc(slot_free, 2)
                    pe.sem_inc(taken, 2)
                    with pe.Fori(0, KD // 2) as i:
                        for j in range(2):
                            pe.wait_ge(loaded[j], i * 96 + 96)
                            for g, (_, y) in enumerate(branches):
                                n = 3 * j + g
                                pe.wait_ge(taken, i * 6 + (n + 1))
                                pair = 2 * (n % 2)
                                for k in range(KD):
                                    for b, e in spans(lo):
                                        pe.matmul(ps[:, pair, LC + b:LC + e], wg[:, j, g, k, :], self.hT[:, k, b:e], start=(k == 0), stop=(k == KD - 1))
                                for k in range(HB):
                                    for b, e in spans(lo):
                                        last = pe.matmul(ps[:, pair + 1, LC + b:LC + e], wb[:, j, g, k, :], y[:, k, b:e], start=(k == 0), stop=(k == HB - 1))
                                last.then_inc(multiplied, 1)
                            pe.wait_ge(multiplied, i * 6 + (3 * j + 3))
                            pe.sem_inc(slot_free, 1)

                @block.scalar
                def _(act):
                    with act.Fori(0, KD // 2) as i:
                        for n in range(6):
                            act.wait_ge(multiplied, i * 6 + (n + 1))
                            act.activation(sg[:, n % 2, lo:], ps[:, 2 * (n % 2), LC + lo:], ACT.Sigmoid).then_inc(opened, 1)

                @block.vector
                def _(dve):
                    step = Steps(dve, own)
                    with dve.Fori(0, KD // 2) as i:
                        step.loop(i, 4)
                        for j in range(2):
                            for g in range(3):
                                n = 3 * j + g
                                dve.wait_ge(opened, i * 6 + (n + 1))
                                dve.tensor_tensor(part[:, g, lo:], sg[:, n % 2, lo:], ps[:, 2 * (n % 2) + 1, LC + lo:], ALU.mult).then_inc(taken, 1)
                            dve.wait_ge(taken, i * 6 + (3 * j + 2 + 2))
                            step(dve.tensor_tensor(acc[:, lo:], part[:, 0, lo:], part[:, 1, lo:], ALU.add))
                            dve.wait_ge(taken, i * 6 + (3 * j + 3 + 2))
                            step.settle()
                            step(dve.tensor_tensor(yT[:, i * 2 + j, lo:], acc[:, lo:], part[:, 2, lo:], ALU.add))
                        step.end(KD // 2)

    def add_mixed(self, l, yT, lo):
        with Stage(self) as s:
            block_done, ps_free = s.signals(2)
            with self.nc.Block() as block:
                self.project(s, block, self.a["w_out"][l].rearrange("(k p) n -> p k n", p=P), yT, KD, lo, block_done, ps_free)

                @block.vector
                def _(dve):
                    with dve.Fori(0, KD // 2) as i:
                        for j in range(2):
                            dve.wait_ge(block_done, i * 2 + (j + 1))
                            for b, e, kind in KIND_RANGE:
                                if e > lo:
                                    last = dve.scalar_tensor_tensor(self.xT[:, i * 2 + j, b:e], self.ps[:, j, LC + b:LC + e],
                                                                    self.modT[:, i * 2 + (2 * KD + j), kind:kind + 1],
                                                                    self.xT[:, i * 2 + j, b:e], ALU.mult, ALU.add)
                            last.then_inc(ps_free, 1)

    def head_gain(self, src, ones, gain, lo, root):
        def finish(dve, step, b, r):
            return dve.scalar_tensor_tensor(src[:, b, lo:], src[:, b, lo:], gain, r[:, lo:], ALU.mult, ALU.mult)
        self.head_norm(src, ones, HEADS, lo, root, finish)

    def gated_out(self, oaT, szT, lo):
        def finish(dve, step, b, r):
            step(dve.tensor_tensor(oaT[:, b, lo:], oaT[:, b, lo:], r[:, lo:], ALU.mult))
            step.settle()
            return dve.scalar_tensor_tensor(oaT[:, b, lo:], oaT[:, b, lo:], self.cols[:, 3:4], szT[:, b, lo:], ALU.mult, ALU.mult)
        self.head_norm(oaT, "ones", HEADS, lo, lambda b: (1.0 / P, self.eps[:, 0:1]), finish)

    def mixers(self, l, lo):
        nc = self.nc
        lam_init = 0.8 - 0.6 * math.exp(-0.3 * l)
        with ExitStack() as outer:
            def sb(st, name, shape):
                return st.enter_context(nc.sbuf_tensor(f"{name}_{l}", shape, F32))
            oaT = sb(outer, "oaT", [P, HEADS, T])
            with ExitStack() as st:
                qkvT = sb(st, "qkvT", [P, 3 * HEADS, T])
                betaT = sb(st, "betaT", [2 * HEADS, T])
                gcT = [sb(st, f"gcT{d}", [HEADS, T]) for d in range(2)]
                beta_nat, gc_nat, kscale = (sb(st, n, [P, TILES, 2 * HEADS]) for n in ("beta_nat", "gc_nat", "kscale"))
                self.gdn_qkv(l, qkvT)
                self.gdn_unit(qkvT)
                self.gdn_gates(l, betaT, gcT, beta_nat, gc_nat, kscale)
                self.gdn_scan(qkvT, oaT, betaT, gcT, beta_nat, gc_nat, kscale)
            ybT = sb(outer, "ybT", [P, HEADS, T])
            ycT = sb(outer, "ycT", [P, HEADS, T])
            with ExitStack() as st:
                szT, qT, kT = (sb(st, n, [P, HEADS, T]) for n in ("szT", "qT", "kT"))
                vda, vhat = (sb(st, n, [P, TILES, HEADS * P]) for n in ("vda", "vhat"))
                lam = sb(st, "lam", [P, 1])
                self.columns(l, ((C_Z, ACT.Silu, szT, lo), (C_U, ACT.Gelu_apprx_tanh, ybT, lo), (C_Q, ACT.Copy, qT, lo), (C_K, ACT.Copy, kT, 0)), lo)
                self.gated_out(oaT, szT, lo)
                self.values(l, vda, vhat, lo)
                self.chunk_mlp(l, ybT, vhat, lo)
                root = lambda b: (1.0 / DH, self.eps[:, 0:1])
                self.head_gain(qT, "blockones", self.cols[:, 0:1], lo, root)
                self.head_gain(kT, "blockones", self.cols[:, 1:2], 0, root)
                self.rotate(l, lam_init, qT, kT, lam)
                self.attend(qT, kT, vda, lam, ycT, lo)
                out = 1.0 - lam_init
                self.head_gain(ycT, "ones", self.cols[:, 2:3], lo, lambda b: (1.0 / P / out ** 2, self.eps[:, 4 + l:5 + l]))
            yT = sb(outer, "yT", [P, KD, T])
            self.merge(l, oaT, ybT, ycT, yT, lo)
            self.add_mixed(l, yT, lo)

    def peer_queries(self, l, qpT, lo):
        with Stage(self) as s:
            block_done, ps_free = s.signals(2)
            NB = 2 * PH
            with self.nc.Block() as block:
                self.project(s, block, self.a["peer_w_q"][l].rearrange("(k p) n -> p k n", p=P), self.hT, NB, lo, block_done, ps_free)

                @block.scalar
                def _(act):
                    with act.Fori(0, NB // 2) as i:
                        for j in range(2):
                            hold(act, block_done, i * 2 + (j + 1))
                            act.activation(qpT[:, i * 2 + j, lo:], self.ps[:, j, LC + lo:], ACT.Copy).then_inc(ps_free, 1)

    def peer_select(self, l, qpT, picks, gates, lo):
        nc, ps = self.nc, self.ps
        NB = 2 * PH
        NEG = -3.0e38
        first = lo // P
        HK = PH * TOPK
        with Stage(self) as s:
            keys_in, turned, keys_flat, staged, scored, copied, sc_free, exps, own = s.signals(9)
            kn = s.sb("kn", [P, NB, P])
            kT = s.sb("kT", [P, NB, P])
            qs = s.sb("qs", [P, NB, P])
            sc = s.sb("sc", [P, NB, NKEYS])
            sc2 = s.sb("sc2", [P, NB, NKEYS])
            val = s.sb("val", [P, NB, TOPK])
            ix = s.sb("ix", [P, NB, TOPK], U32)
            ixf = s.sb("ixf", [P, NB, TOPK])
            cand = s.sb("cand", [P, PH, TOPK * TOPK])
            best = s.sb("best", [P, PH, TOPK])
            pos = s.sb("pos", [P, HK], U32)
            side = s.sb("side", [P, 2, HK], U32)
            sidef = s.sb("sidef", [P, 2, HK])
            got = s.sb("got", [P, 2, HK])
            row = s.sb("row", [P, HK])
            ex = s.sb("ex", [P, PH, TOPK])
            tot = s.sb("tot", [P, PH])
            rt = s.sb("rt", [P, PH])
            cand2 = sc2[:, :, :].rearrange("p b n -> p (b n)").rearrange("p (h c) -> p h c", h=PH)
            hot = cand[:, :, :].rearrange("p h c -> p (h c)")
            with nc.Block() as block:
                @block.sync
                def _(sp):
                    sp.dma_start(kn[:, :, :], self.a["peer_subkeys"][l].rearrange("h i n d -> n (h i) d")).then_inc(keys_in, 16)

                @block.tensor
                def _(pe):
                    pe.wait_ge(keys_in, 16)
                    for b in range(NB):
                        last = pe.transpose(ps[:, b // 8, (b % 8) * P:(b % 8 + 1) * P], kn[:, b, :], self.c("ident"))
                    last.then_inc(turned, 1)
                    pe.wait_ge(keys_flat, 1)
                    with pe.Fori(first, TILES) as i:
                        pe.wait_ge(staged, i - first + 1)
                        for b in range(NB):
                            last = pe.matmul(ps[:, b // 8, (b % 8) * P:(b % 8 + 1) * P], qs[:, b, :], kT[:, b, :], start=True, stop=True)
                        last.then_inc(scored, 1)

                @block.scalar
                def _(act):
                    act.wait_ge(turned, 1)
                    for n in range(2):
                        last = act.activation(kT[:, 8 * n:8 * n + 8, :], ps[:, n].rearrange("p (b c) -> p b c", b=8), ACT.Copy)
                    last.then_inc(keys_flat, 1)
                    with act.Fori(first, TILES) as i:
                        act.activation(qs[:, :, :], qpT[:, :, bass.ts(i, P)], ACT.Copy).then_inc(staged, 1)
                        act.wait_ge(scored, i - first + 1)
                        act.wait_ge(sc_free, i - first + 1)
                        for n in range(2):
                            last = act.activation(sc[:, 8 * n:8 * n + 8, :], ps[:, n].rearrange("p (b c) -> p b c", b=8), ACT.Copy)
                        last.then_inc(copied, 1)
                        act.wait_ge(exps, i * 2 - 2 * first + 1)
                        act.activation(ex[:, :, :], ex[:, :, :], ACT.Exp).then_inc(exps, 1)

                @block.vector
                def _(dve):
                    step = Steps(dve, own)
                    dve.sem_inc(sc_free, 1)
                    with dve.Fori(first, TILES) as i:
                        step.loop(i - first, 5 * NB - 1 + 5 * PH + 16)
                        hold(dve, copied, i - first + 1)
                        for b in range(NB):
                            step(dve.max(val[:, b, 0:8], sc[:, b, :]))
                        step.settle(apart=True)
                        for b in range(NB):
                            step(dve.match_replace(sc2[:, b, :], val[:, b, 0:8], sc[:, b, :], NEG))
                        for b in range(NB):
                            ins = dve.max_index(ix[:, b, 0:8], val[:, b, 0:8], sc[:, b, :])
                            if b < NB - 1:
                                step(ins)
                            else:
                                ins.then_inc(sc_free, 1)
                        step.settle(apart=True)
                        for b in range(NB):
                            step(dve.max(val[:, b, 8:16], sc2[:, b, :]))
                        step.settle(apart=True)
                        for b in range(NB):
                            step(dve.max_index(ix[:, b, 8:16], val[:, b, 8:16], sc2[:, b, :]))
                        both = val[:, :, :].rearrange("p (h i) n -> p i h n", i=2)
                        first_side = both[:, 0].rearrange("p h (n o) -> p h n o", o=1).broadcast_to([P, PH, TOPK, TOPK])
                        second = both[:, 1].rearrange("p h (o n) -> p h o n", o=1).broadcast_to([P, PH, TOPK, TOPK])
                        c4 = cand[:, :, :].rearrange("p h (a b) -> p h a b", a=TOPK)
                        step(dve.tensor_tensor(c4, first_side, second, ALU.add))
                        step.settle()
                        step(dve.tensor_copy(ixf[:, :, :], ix[:, :, :]))
                        for h in range(PH):
                            step(dve.max(best[:, h, 0:8], cand[:, h, :]))
                        step.settle(apart=True)
                        for h in range(PH):
                            step(dve.match_replace(cand2[:, h, :], best[:, h, 0:8], cand[:, h, :], NEG))
                        for h in range(PH):
                            step(dve.max_index(pos[:, TOPK * h:TOPK * h + 8], best[:, h, 0:8], cand[:, h, :]))
                        step.settle(apart=True)
                        for h in range(PH):
                            step(dve.max(best[:, h, 8:16], cand2[:, h, :]))
                        step.settle(apart=True)
                        for h in range(PH):
                            step(dve.max_index(pos[:, TOPK * h + 8:TOPK * h + 16], best[:, h, 8:16], cand2[:, h, :]))
                        dve.tensor_tensor(ex[:, :, :], best[:, :, :], best[:, :, 0:1].broadcast_to([P, PH, TOPK]), ALU.subtract).then_inc(exps, 1)
                        step.settle()
                        step(dve.tensor_single_scalar(side[:, 0], pos[:, :], 4, ALU.logical_shift_right))
                        step(dve.tensor_single_scalar(side[:, 1], pos[:, :], 15, ALU.bitwise_and))
                        step.settle()
                        step(dve.tensor_copy(sidef[:, :, :], side[:, :, :]))
                        step.settle()
                        for m in range(2):
                            h3 = hot.rearrange("p (k n) -> p k n", n=TOPK)
                            step(dve.tensor_tensor(h3, each(sidef[:, m], TOPK), over(self.c("iota"), HK), ALU.is_equal))
                            step.settle()
                            h4 = hot.rearrange("p (h k n) -> p h k n", h=PH, n=TOPK)
                            keys = ixf[:, :, :].rearrange("p (h i) n -> p i h n", i=2)[:, m].rearrange("p h (o n) -> p h o n", o=1).broadcast_to([P, PH, TOPK, TOPK])
                            step(dve.tensor_tensor(h4, h4, keys, ALU.mult))
                            step.settle()
                            step(dve.reduce_sum(got[:, m], h3, axis=AX))
                            step.settle()
                        step(dve.scalar_tensor_tensor(row[:, :], got[:, 0], float(NKEYS), got[:, 1], ALU.mult, ALU.add))
                        step.settle(apart=True)
                        step(dve.tensor_copy(picks[:, i, :], row[:, :]))
                        dve.wait_ge(exps, i * 2 - 2 * first + 2)
                        step(dve.reduce_sum(tot[:, :], ex[:, :, :], axis=AX))
                        step.settle()
                        step(dve.reciprocal(rt[:, :], tot[:, :]))
                        step.settle(apart=True)
                        step(dve.tensor_tensor(gates[:, i, :].rearrange("p (h n) -> p h n", h=PH), ex[:, :, :], each(rt[:, :], TOPK), ALU.mult))
                        step.end(TILES - first)

    def peer_experts(self, l, picks, gates, lo):
        nc, ps = self.nc, self.ps
        NBATCH = PICKS // BATCH
        first = lo // P
        gathered, before = self.gathered, self.gathered_count
        self.gathered_count += 16 * 2 * NBATCH * (TILES - first)
        tables = (self.a["peer_u"], self.a["peer_v"])
        with Stage(self) as s:
            used, staged, rows_ready, h_copied, h_turned, h_ready, dotted, gelued, own, summed, sum_turned, added = s.signals(12)
            ring = s.sb("ring", [P, BATCH, D])
            ist = s.sb("ist", [P, 2, BATCH], U32)
            hs = s.sb("hs", [P, KD, P])
            hn = s.sb("hn", [P, KD, P])
            dots = s.sb("dots", [P, 2, BATCH])
            act_in = s.sb("act_in", [P, PICKS])
            act_out = s.sb("act_out", [P, PICKS])
            wgt = s.sb("wgt", [P, PICKS])
            acc = s.sb("acc", [P, 2, D])
            accs = s.sb("accs", [P, D])
            tmp = s.sb("tmp", [P, KD, P])

            def token_major(ap):
                return ap.rearrange("p k c -> p (k c)")

            loops = [(max(b // P, first), e // P, kind) for b, e, kind in reversed(KIND_RANGE) if e // P > first]

            with nc.Block() as block:
                @block.gpsimd
                def _(pool):
                    with pool.Fori(first, TILES) as i:
                        for part, table in enumerate(tables):
                            with pool.Fori(0, NBATCH // 2) as kb:
                                for h in range(2):
                                    batch = (i - first) * (2 * NBATCH) + kb * 2 + (part * NBATCH + h)
                                    pool.tensor_copy(ist[:, h], picks[:, i, bass.ts(kb * 2 + h, BATCH)]).then_inc(staged, 1)
                                    hold(pool, staged, batch + 1)
                                    for j in range(BATCH):
                                        hold(pool, used, batch * BATCH + (j + 1))
                                        pool.indirect_dma_start(out=ring[:, j, :], out_offset=None, in_=table.rearrange("l e d -> (l e) d"),
                                                                in_offset=bass.IndirectOffsetOnAxis(ap=ist[:, h, j:j + 1], axis=0),
                                                                element_offset=l * EXPERTS * D).then_inc(gathered[j], 16)

                @block.scalar
                def _(act):
                    def prepare(i):
                        act.activation(hs[:, :, :], self.hT[:, :, bass.ts(i, P)], ACT.Copy).then_inc(h_copied, 1)
                        act.wait_ge(h_turned, i - first + 1)
                        act.activation(token_major(hn[:, :, :]), ps[:, 0, :], ACT.Copy).then_inc(h_ready, 1)

                    prepare(first)
                    with act.Fori(first, TILES - 1) as i:
                        act.wait_ge(dotted, i - first + 1)
                        act.activation(act_out[:, :], act_in[:, :], ACT.Gelu_apprx_tanh).then_inc(gelued, 1)
                        prepare(i + 1)
                    act.wait_ge(dotted, TILES - first)
                    act.activation(act_out[:, :], act_in[:, :], ACT.Gelu_apprx_tanh).then_inc(gelued, 1)

                @block.tensor
                def _(pe):
                    def turn_h(i):
                        pe.wait_ge(h_copied, i - first + 1)
                        for k in range(KD):
                            last = pe.transpose(ps[:, 0, k * P:(k + 1) * P], hs[:, k, :], self.c("ident"))
                        last.then_inc(h_turned, 1)

                    def turn_sum(i):
                        pe.wait_ge(summed, i - first + 1)
                        for k in range(KD):
                            last = pe.transpose(ps[:, 1, k * P:(k + 1) * P], accs[:, k * P:(k + 1) * P], self.c("ident"))
                        last.then_inc(sum_turned, 1)

                    turn_h(first)
                    with pe.Fori(first, TILES - 1) as i:
                        turn_h(i + 1)
                        turn_sum(i)
                    turn_sum(TILES - 1)

                @block.vector
                def _(dve):
                    dve.sem_inc(used, BATCH)
                    half = NBATCH // 2
                    for begin, end, kind in loops:
                        with dve.Fori(begin, end) as i:
                            hold(dve, h_ready, i - first + 1)
                            with dve.Fori(0, half) as kb:
                                for h in range(2):
                                    batch = (i - first) * (2 * NBATCH) + kb * 2 + h
                                    for j in range(BATCH):
                                        dve.wait_ge(gathered[j], batch * 16 + (before + 16))
                                        dve.tensor_tensor_reduce(out=ring[:, j, :], in0=ring[:, j, :], in1=token_major(hn[:, :, :]), scale=1.0, scalar=0.0,
                                                                 op0=ALU.mult, op1=ALU.add, accum_out=dots[:, h, j:j + 1]).then_inc(used, 1)
                                    hold(dve, used, batch * BATCH + 2 * BATCH)
                                    dve.tensor_copy(act_in[:, bass.ts(kb * 2 + h, BATCH)], dots[:, h]).then_inc(own, 1)
                            hold(dve, own, (i - first) * (NBATCH + 3) + NBATCH)
                            dve.sem_inc(dotted, 1)
                            dve.memset(acc[:, :, :], 0.0).then_inc(own, 1)
                            hold(dve, gelued, i - first + 1)
                            dve.tensor_tensor(wgt[:, :], act_out[:, :], gates[:, i, :], ALU.mult).then_inc(own, 1)
                            hold(dve, own, (i - first) * (NBATCH + 3) + (NBATCH + 2))
                            with dve.Fori(0, half) as kb:
                                for h in range(2):
                                    batch = (i - first) * (2 * NBATCH) + kb * 2 + (NBATCH + h)
                                    for j in range(BATCH):
                                        dve.wait_ge(used, batch * BATCH + (j + BATCH - 1))
                                        dve.wait_ge(gathered[j], batch * 16 + (before + 16))
                                        dve.scalar_tensor_tensor(acc[:, j % 2], ring[:, j, :], wgt[:, :].rearrange("p (b j) -> p b j", j=BATCH)[:, kb * 2 + h, j:j + 1],
                                                                 acc[:, j % 2], ALU.mult, ALU.add).then_inc(used, 1)
                            hold(dve, used, (i - first) * (2 * PICKS) + (2 * PICKS + BATCH))
                            dve.tensor_tensor(accs[:, :], acc[:, 0], acc[:, 1], ALU.add).then_inc(summed, 1)
                            hold(dve, sum_turned, i - first + 1)
                            dve.tensor_tensor(tmp[:, :, :], ps[:, 1, :].rearrange("p (k c) -> p k c", k=KD),
                                              each(self.modT[:, 5 * KD:6 * KD, kind], P), ALU.mult).then_inc(own, 1)
                            hold(dve, own, (i - first) * (NBATCH + 3) + (NBATCH + 3))
                            x_tile = self.xT[:, :, bass.ts(i, P)]
                            dve.tensor_tensor(x_tile, x_tile, tmp[:, :, :], ALU.add)

    def experts(self, l, lo):
        with ExitStack() as st:
            def sb(st, name, shape, dt=F32):
                return st.enter_context(self.nc.sbuf_tensor(f"{name}_{l}", shape, dt))
            picks = sb(st, "picks", [P, TILES, PICKS], U32)
            gates = sb(st, "gates", [P, TILES, PICKS])
            with ExitStack() as inner:
                qpT = sb(inner, "qpT", [P, 2 * PH, T])
                self.peer_queries(l, qpT, lo)
                self.peer_select(l, qpT, picks, gates, lo)
            self.peer_experts(l, picks, gates, lo)

    def store(self):
        nc, ps = self.nc, self.ps
        with Stage(self) as s:
            turned, flat, stored = s.signals(3)
            xn = s.sb("xn", [P, TILES - CTILES, D])
            with nc.Block() as block:
                @block.tensor
                def _(pe):
                    for t in range(TILES - CTILES):
                        for k in range(KD):
                            last = pe.transpose(ps[:, t, k * P:(k + 1) * P], self.xT[:, k, LC + t * P:LC + (t + 1) * P], self.c("ident"))
                        last.then_inc(turned, 1)

                @block.vector
                def _(dve):
                    for t in range(TILES - CTILES):
                        dve.wait_ge(turned, t + 1)
                        dve.tensor_copy(xn[:, t, :], ps[:, t, :]).then_inc(flat, 1)

                @block.sync
                def _(sp):
                    for t in range(TILES - CTILES):
                        sp.wait_ge(flat, t + 1)
                        sp.dma_start(self.out[0, t * P:(t + 1) * P, :], xn[:, t, :]).then_inc(stored, 16)
                    sp.wait_ge(stored, 16 * (TILES - CTILES))


def hybrid_kernel(nc, a, out):
    with ExitStack() as st:
        k = Kernel(nc, a, out, st)
        k.setup()
        for l in range(DEPTH):
            lo = LC if l == DEPTH - 1 else 0
            k.modulation(l)
            k.norm(k.gain1, 0)
            k.mixers(l, lo)
            k.norm(k.gain2, 3, lo)
            k.experts(l, lo)
        k.store()


def kernel(**inputs):
    import concourse.bacc as bacc
    from concourse.bass_utils import run_bass_kernel_spmd

    nc = bacc.Bacc("TRN2", target_bir_lowering=False, num_devices=1)
    arrays = {name: np.ascontiguousarray(value) for name, value in inputs.items()}
    a = {name: nc.dram_tensor(name, value.shape, mybir.dt.from_np(value.dtype), kind="ExternalInput").ap()
         for name, value in arrays.items()}
    out = nc.dram_tensor("out", arrays["x"].shape, F32, kind="ExternalOutput").ap()
    hybrid_kernel(nc, a, out)
    return run_bass_kernel_spmd(nc, [arrays], core_ids=[0]).results[0]["out"]
```

```python
import math
from contextlib import ExitStack

import numpy as np

import concourse.bass as bass
from concourse import mybir

F32 = mybir.dt.float32
U32 = mybir.dt.uint32
ALU = mybir.AluOpType
ACT = mybir.ActivationFunctionType
AX = mybir.AxisListType.X

P = 128
D = 1024
KD = D // P
LC, LX = 256, 512
T = LC + LX
TILES, CTILES = T // P, LC // P
EPS = 1e-6
DEPTH = 2
HEADS = 4
DH = 64
PH, TOPK, NKEYS = 8, 16, 128
PICKS = PH * TOPK
EXPERTS = NKEYS * NKEYS
LEVELS = 7
C_QKV, C_Z, C_BA, C_U, C_V, C_Q, C_K, C_DV, C_G = 0, 1536, 2048, 2064, 2576, 3088, 3600, 4112, 4624
PAD = 2
CW = LC + LX + 6 * PAD - 4
KIND_RANGE = ((LC, T, 0), (0, LC, 1))
BATCH = 8


def constants():
    i = np.arange(P)
    ident = np.eye(P, dtype=np.float32)
    upper = (i[:, None] <= i[None, :]).astype(np.float32)
    masks = np.zeros((P, 2, LEVELS, P), np.float32)
    for lv in range(LEVELS):
        s = 1 << lv
        low = (i[:, None] // s == i[None, :] // s + 1) & (i[:, None] // (2 * s) == i[None, :] // (2 * s))
        masks[:, 0, lv] = low
        masks[:, 1, lv] = low.T
    perm = np.zeros((P, P), np.float32)
    for b in (0, DH):
        for d in range(DH // 2):
            perm[b + d + DH // 2, b + d] = -1.0
            perm[b + d, b + d + DH // 2] = 1.0
    blockones = (i[:, None] // DH == i[None, :] // DH).astype(np.float32)
    sel = np.zeros((P, 8, P), np.float32)
    for j in range(8):
        sel[j, j] = 1.0
    inv = (10000.0 ** (-np.arange(DH // 4, dtype=np.float32) / np.float32(DH // 4))).astype(np.float32)
    t = np.arange(LX)
    ang = np.concatenate([(t // 64).astype(np.float32)[:, None] * inv,
                          (t % 64).astype(np.float32)[:, None] * inv], axis=-1)
    ang = np.tile(ang.T, (4, 1))
    cols = [("ident", ident), ("upper", upper), ("lower", upper.T), ("perm", perm), ("blockones", blockones),
            ("ident4", np.tile(ident, (1, HEADS))), ("masks", masks.reshape(P, -1)), ("sel", sel.reshape(P, -1)),
            ("cos", np.cos(ang)), ("sin", np.sin(ang)), ("ones", np.ones((P, P))),
            ("iota", np.tile(np.arange(TOPK), (P, 1)))]
    at, n = {}, 0
    for name, a in cols:
        at[name] = (n, a.shape[1])
        n += a.shape[1]
    return np.concatenate([np.asarray(a, np.float32) for _, a in cols], axis=1), at


def spans(lo):
    return ((0, LC), (LC, T)) if lo < LC else ((LC, T),)


class Steps:

    def __init__(self, eng, sem):
        self.eng, self.sem, self.n, self.off = eng, sem, 0, None

    def __call__(self, instruction):
        instruction.then_inc(self.sem, 1)
        self.n += 1

    def loop(self, i, per):
        self.off, self.n0, self.per = i * per, self.n, per

    def begin(self, base):
        self.off, self.n = base, 0

    def end(self, trips):
        assert self.n - self.n0 == self.per, (self.n - self.n0, self.per)
        self.n, self.off = self.n0 + self.per * trips, None

    def settle(self, back=0, apart=False):
        if self.off is None:
            self.eng.wait_ge(self.sem, self.n - back)
        else:
            self.eng.wait_ge(self.sem, self.off + (self.n - back))
            if apart:
                self.eng.nop(nofuse=True)


def hold(eng, sem, value):
    eng.wait_ge(sem, value)
    eng.nop(nofuse=True)


def over(ap, n):
    return ap.rearrange("p (o c) -> p o c", o=1).broadcast_to([ap.shape[0], n, ap.shape[1]])


def each(ap, n):
    return ap.rearrange("p (c o) -> p c o", o=1).broadcast_to([ap.shape[0], ap.shape[1], n])


class Stage:

    def __init__(self, k):
        self.k, self.used = k, 0

    def __enter__(self):
        self.st = ExitStack()
        self.st.__enter__()
        return self

    def sb(self, name, shape, dt=F32):
        self.k.serial += 1
        return self.st.enter_context(self.k.nc.sbuf_tensor(f"{name}_{self.k.serial}", shape, dt))

    def signals(self, n):
        self.used += n
        return self.k.sems[self.used - n:self.used]

    def __exit__(self, *a):
        self.st.__exit__(*a)
        first = self.k.sems[0].num
        self.k.nc.all_engine_barrier(sems_to_clear=range(first, first + self.used))


class Kernel:
    def __init__(self, nc, a, out, st):
        self.nc, self.a, self.out, self.serial = nc, a, out, 0
        self.sems = [nc.alloc_semaphore(f"stage_signal_{i}") for i in range(40)]
        assert [x.num for x in self.sems] == list(range(self.sems[0].num, self.sems[0].num + 40))

        self.gathered = [nc.alloc_semaphore(f"gathered_{j}") for j in range(BATCH)]
        self.gathered_count = 0

        def sb(name, shape, dt=F32):
            return st.enter_context(nc.sbuf_tensor(name, shape, dt))
        table, self.at = constants()
        self.const_dram = nc.inline_tensor(table)
        self.consts = sb("consts", [P, table.shape[1]])
        self.xT = sb("xT", [P, KD, T])
        self.hT = sb("hT", [P, KD, T])
        self.sT = sb("sT", [P, KD, 2])
        self.modT = sb("modT", [P, 6 * KD, 2])
        self.gain1 = sb("gain1", [P, KD, 2])
        self.gain2 = sb("gain2", [P, KD, 2])
        self.cols = sb("cols", [P, 4])
        self.inv_root = sb("inv_root", [P, T])
        self.eps = sb("eps", [P, 4 + DEPTH])
        self.ps = st.enter_context(nc.psum_tensor("ps", [P, 4, 2 * 512], F32))

    def c(self, name):
        at, n = self.at[name]
        return self.consts[:, at:at + n]

    def setup(self):
        nc, a, ps = self.nc, self.a, self.ps
        with Stage(self) as s:
            consts_in, c_in, x_in, turned, copied_even, copied_odd = s.signals(6)
            xn = s.sb("xn", [P, TILES, D])
            cT = s.sb("cT", [P, KD, 2])
            with nc.Block() as block:
                @block.sync
                def _(sp):
                    sp.dma_start(self.consts[:, :], self.const_dram[:, :]).then_inc(consts_in, 16)
                    sp.dma_start(xn[:, 0:CTILES, :], a["ctx"].rearrange("o (t p) d -> p (o t) d", p=P)).then_inc(x_in, 16)
                    sp.dma_start(xn[:, CTILES:, :], a["x"].rearrange("o (t p) d -> p (o t) d", p=P)).then_inc(x_in, 16)

                @block.scalar
                def _(act):
                    with nc.allow_non_contiguous_dma(reason="1024 elements"):
                        act.dma_start(cT[:, :, 0], a["c"].rearrange("o (k p) -> p (o k)", p=P)).then_inc(c_in, 16)
                        act.dma_start(cT[:, :, 1], a["c_ctx"].rearrange("(k p) -> p k", p=P)).then_inc(c_in, 16)
                    act.wait_ge(c_in, 32)
                    act.activation(self.sT[:, :, :], cT[:, :, :], ACT.Silu)
                    for k in range(1, KD, 2):
                        act.wait_ge(turned, k + 1)
                        act.activation(self.xT[:, k, :], ps[:, k % 4, LC:], ACT.Copy).then_inc(copied_odd, 1)

                @block.tensor
                def _(pe):
                    pe.wait_ge(consts_in, 16)
                    pe.wait_ge(x_in, 32)
                    for k in range(KD):
                        if k >= 4:
                            pe.wait_ge(copied_odd if k % 2 else copied_even, (k - 4) // 2 + 1)
                        for t in range(TILES):
                            last = pe.transpose(ps[:, k % 4, LC + t * P:LC + (t + 1) * P],
                                                xn[:, t, k * P:(k + 1) * P], self.c("ident"))
                        last.then_inc(turned, 1)

                @block.vector
                def _(dve):
                    for j, v in enumerate((EPS, EPS, P * EPS, 1.0) + tuple(EPS / (0.2 + 0.6 * math.exp(-0.3 * l)) ** 2 for l in range(DEPTH))):
                        dve.memset(self.eps[:, j:j + 1], v)
                    for k in range(0, KD, 2):
                        dve.wait_ge(turned, k + 1)
                        dve.tensor_copy(self.xT[:, k, :], ps[:, k % 4, LC:]).then_inc(copied_even, 1)

    def modulation(self, l):
        nc, a, ps = self.nc, self.a, self.ps
        CH = 512
        NCH = 6 * D // CH
        with Stage(self) as s:
            loaded = s.signals(2)
            small_in, slot_free, multiplied, own, ps_free, turned = s.signals(6)
            squared, summed, logged = s.signals(3)
            sq = s.sb("sq", [P, 2, T])
            w = s.sb("w", [P, 2, KD, CH])
            rows = s.sb("rows", [2, 6 * D])
            bT = s.sb("bT", [P, 6 * KD])
            gT = s.sb("gT", [P, 2, KD])
            src = a["w_mod"][l].rearrange("(k p) n -> p k n", p=P)
            with nc.Block() as block:
                @block.sync
                def _(sp):
                    with sp.Fori(0, NCH // 2) as i:
                        for j in range(2):
                            sp.wait_ge(slot_free, i * 2 + (j + 1))
                            sp.dma_start(w[:, j], src[:, :, bass.ts(i * 2 + j, CH)]).then_inc(loaded[j], 16)

                @block.scalar
                def _(act):
                    with nc.allow_non_contiguous_dma(reason="vectors turned to columns"):
                        act.dma_start(bT[:, :], a["b_mod"][l].rearrange("(k p) -> p k", p=P)).then_inc(small_in, 16)
                        act.dma_start(gT[:, 0], a["norm1_g"][l].rearrange("(k p) -> p k", p=P)).then_inc(small_in, 16)
                        act.dma_start(gT[:, 1], a["norm2_g"][l].rearrange("(k p) -> p k", p=P)).then_inc(small_in, 16)
                        for j, name in enumerate(("da_q_norm_g", "da_k_norm_g")):
                            for half in range(2):
                                act.dma_start(self.cols[half * DH:(half + 1) * DH, j:j + 1], a[name][l].rearrange("(p o) -> p o", o=1)).then_inc(small_in, 16)
                        for j, name in enumerate(("da_subln_g", "gdn_out_norm_g")):
                            act.dma_start(self.cols[:, 2 + j:3 + j], a[name][l].rearrange("(p o) -> p o", o=1)).then_inc(small_in, 16)
                    self.invert_root(act, 3, sq, squared, summed, logged, None, 0)

                @block.tensor
                def _(pe):
                    pe.sem_inc(slot_free, 2)
                    pe.sem_inc(ps_free, 2)
                    with pe.Fori(0, NCH // 2) as i:
                        for j in range(2):
                            pe.wait_ge(loaded[j], i * 16 + 16)
                            pe.wait_ge(ps_free, i * 2 + (j + 1))
                            for k in range(KD):
                                last = pe.matmul(ps[0:2, j, 0:CH], self.sT[:, k, :], w[:, j, k, :], start=(k == 0), stop=(k == KD - 1))
                            last.then_inc(multiplied, 1)
                            pe.wait_ge(multiplied, i * 2 + (j + 1))
                            pe.sem_inc(slot_free, 1)
                    self.sum_squares(pe, 3, sq, squared, summed, 0)
                    pe.wait_ge(ps_free, NCH + 2)
                    for b in range(6 * KD):
                        last = pe.transpose(ps[:, 2, 2 * b:2 * b + 2], rows[:, b * P:(b + 1) * P], self.c("ident")[0:2, 0:2])
                    last.then_inc(turned, 1)

                @block.vector
                def _(dve):
                    step = Steps(dve, own)
                    with dve.Fori(0, NCH // 2) as i:
                        for j in range(2):
                            hold(dve, multiplied, i * 2 + (j + 1))
                            dve.tensor_copy(rows[:, bass.ts(i * 2 + j, CH)], ps[0:2, j, 0:CH]).then_inc(ps_free, 1)
                    dve.wait_ge(small_in, 9 * 16)
                    dve.wait_ge(turned, 1)
                    step(dve.tensor_tensor(self.modT[:, :, :], ps[:, 2, 0:12 * KD].rearrange("p (b s) -> p b s", s=2), each(bT[:, :], 2), ALU.add))
                    step.settle()
                    for gain, part, which in ((self.gain1, 1, 0), (self.gain2, 4, 1)):
                        step(dve.tensor_scalar(gain[:, :, :], self.modT[:, part * KD:(part + 1) * KD, :], 1.0, None, ALU.add))
                        step.settle()
                        step(dve.tensor_tensor(gain[:, :, :], gain[:, :, :], each(gT[:, which], 2), ALU.mult))

    def sum_squares(self, pe, pair, sq, squared, summed, lo):
        for k in range(KD):
            pe.wait_ge(squared, k + 1)
            for b, e in spans(lo):
                last = pe.matmul(self.ps[:, pair, LC + b:LC + e], self.c("ones"), sq[:, k % 2, b:e],
                                 start=(k == 0), stop=(k == KD - 1))
            last.then_inc(summed, 1)

    def invert_root(self, act, pair, sq, squared, summed, logged, rooted, lo):
        for k in range(KD):
            if k >= 2:
                act.wait_ge(summed, k - 1)
            act.activation(sq[:, k % 2, lo:], self.xT[:, k, lo:], ACT.Square).then_inc(squared, 1)
        act.wait_ge(summed, KD)
        act.activation(sq[:, 0, lo:], self.ps[:, pair, LC + lo:], ACT.Ln, bias=self.eps[:, 0:1], scale=1.0 / D).then_inc(logged, 1)
        act.wait_ge(logged, 1)
        last = act.activation(self.inv_root[:, lo:], sq[:, 0, lo:], ACT.Exp, scale=-0.5)
        if rooted is not None:
            last.then_inc(rooted, 1)

    def norm(self, gain, shift, lo=0, ready=False):
        with Stage(self) as s:
            squared, summed, logged, rooted, scaled, scaled_used = s.signals(6)
            sq = s.sb("sq", [P, 2, T])
            xr = s.sb("xr", [P, 2, T])
            with self.nc.Block() as block:
                @block.scalar
                def _(act):
                    if not ready:
                        self.invert_root(act, 0, sq, squared, summed, logged, rooted, lo)
                    for k in range(KD):
                        act.wait_ge(scaled, k + 1)
                        for b, e, kind in KIND_RANGE:
                            if e > lo:
                                last = act.activation(self.hT[:, k, b:e], xr[:, k % 2, b:e], ACT.Identity,
                                                      bias=self.modT[:, shift * KD + k, kind:kind + 1],
                                                      scale=gain[:, k, kind:kind + 1])
                        last.then_inc(scaled_used, 1)

                if not ready:
                    @block.tensor
                    def _(pe):
                        self.sum_squares(pe, 0, sq, squared, summed, lo)

                @block.vector
                def _(dve):
                    if not ready:
                        dve.wait_ge(rooted, 1)
                    for k in range(KD):
                        if k >= 2:
                            dve.wait_ge(scaled_used, k - 1)
                        dve.tensor_tensor(xr[:, k % 2, lo:], self.xT[:, k, lo:], self.inv_root[:, lo:], ALU.mult).then_inc(scaled, 1)

    def project(self, s, block, w_view, rhs, nblocks, lo, block_done, ps_free, gates=()):
        loaded = s.signals(2)
        slot_free, = s.signals(1)
        w = s.sb("w", [P, 2, KD, 2 * P])
        trips = nblocks // 4

        @block.sync
        def _(sp):
            with sp.Fori(0, trips) as i:
                for j in range(2):
                    sp.wait_ge(slot_free, i * 2 + (j + 1))
                    sp.dma_start(w[:, j], w_view[:, :, bass.ts(i * 2 + j, 2 * P)]).then_inc(loaded[j], 16)

        @block.tensor
        def _(pe):
            pe.sem_inc(slot_free, 2)
            pe.sem_inc(ps_free, 2)
            with pe.Fori(0, trips) as i:
                for j in range(2):
                    pe.wait_ge(loaded[j], i * 16 + 16)
                    for h in range(2):
                        pe.wait_ge(ps_free, i * 4 + (2 * j + h + 1))
                        for k in range(KD):
                            for b, e in spans(lo):
                                last = pe.matmul(self.ps[:, h, LC + b:LC + e], w[:, j, k, h * P:(h + 1) * P],
                                                 rhs[:, k, b:e], start=(k == 0), stop=(k == KD - 1))
                        last.then_inc(block_done, 1)
                    pe.wait_ge(block_done, i * 4 + (2 * j + 2))
                    pe.sem_inc(slot_free, 1)

    def w_in(self, l, col, n):
        return self.a["w_in"][l].rearrange("(k p) n -> p k n", p=P)[:, :, col:col + n]

    def gdn_qkv(self, l, qkvT):
        nc, ps = self.nc, self.ps
        NB = 12
        with Stage(self) as s:
            block_done, ps_free, padded, conved, own, small_in, silud, zeroed = s.signals(8)
            cb = s.sb("cb", [P, CW])
            cv = s.sb("cv", [P, 5, CW - 4])
            taps = s.sb("taps", [P, NB, 5])
            with nc.Block() as block:
                self.project(s, block, self.w_in(l, C_QKV, NB * P), self.hT, NB, 0, block_done, ps_free)

                @block.scalar
                def _(act):
                    with nc.allow_non_contiguous_dma(reason="7680 taps"):
                        for j in range(5):
                            act.dma_start(taps[:, :, j], self.a["gdn_conv_w"][l, j].rearrange("(b p) -> p b", p=P)).then_inc(small_in, 16)
                    act.wait_ge(zeroed, 1)
                    with act.Fori(0, NB // 2) as i:
                        for j in range(2):
                            act.wait_ge(block_done, i * 2 + (j + 1))
                            act.activation(cb[:, PAD:PAD + LC], ps[:, j, LC:2 * LC], ACT.Copy)
                            act.activation(cb[:, 3 * PAD + LC:3 * PAD + T], ps[:, j, 2 * LC:], ACT.Copy).then_inc(padded, 1)
                            hold(act, conved, i * 2 + (j + 1))
                            act.activation(qkvT[:, i * 2 + j, 0:LC], cv[:, 4, 0:LC], ACT.Silu)
                            act.activation(qkvT[:, i * 2 + j, LC:], cv[:, 4, LC + 2 * PAD:], ACT.Silu).then_inc(silud, 1)

                @block.vector
                def _(dve):
                    step = Steps(dve, own)
                    dve.memset(cb[:, :], 0.0).then_inc(zeroed, 1)
                    dve.wait_ge(small_in, 5 * 16)
                    n = CW - 4
                    with dve.Fori(0, NB // 2) as i:
                        step.loop(i, 8)
                        for j in range(2):
                            hold(dve, padded, i * 2 + (j + 1))
                            dve.sem_inc(ps_free, 1)
                            dve.tensor_scalar(cv[:, 0], cb[:, 0:n], taps[:, i * 2 + j, 0:1], None, ALU.mult).then_inc(own, 1)
                            step.n += 1
                            for tap in range(1, 5):
                                step.settle()
                                ins = dve.scalar_tensor_tensor(cv[:, tap], cb[:, tap:tap + n], taps[:, i * 2 + j, tap:tap + 1],
                                                               cv[:, tap - 1], ALU.mult, ALU.add)
                                if tap < 4:
                                    step(ins)
                                else:
                                    ins.then_inc(conved, 1)
                        step.end(NB // 2)

    def gdn_gates(self, l, qkvT, betaT, gcT, beta_nat, gc_nat, kscale):
        nc, ps = self.nc, self.ps
        with Stage(self) as s:
            small_in, made, own, own_act, turned, flat, summed = s.signals(7)
            squared, squares_summed, logged, inverted, scaled = s.signals(5)
            sq = s.sb("sq", [P, 4, T])
            NU = 2 * HEADS
            w = s.sb("w", [P, KD, 16])
            cols = s.sb("cols", [8, 4])
            gx = s.sb("gx", [8, T])
            ga = s.sb("ga", [8, T])
            ge = s.sb("ge", [8, T])
            gl = s.sb("gl", [8, T])
            gm = s.sb("gm", [8, T])
            gT = s.sb("gT", [8, T])
            gn = s.sb("gn", [P, 2, TILES, HEADS])
            eg = s.sb("eg", [P, TILES, 8])
            with nc.Block() as block:
                @block.sync
                def _(sp):
                    with nc.allow_non_contiguous_dma(reason="16 columns, 16 numbers"):
                        sp.dma_start(w[:, :, :], self.w_in(l, C_BA, 16)).then_inc(small_in, 16)
                        sp.dma_start(cols[:, 0:1], self.a["gdn_dt_bias"][l].rearrange("d (h o) -> (d h) o", o=1)).then_inc(small_in, 16)
                        sp.dma_start(cols[:, 1:2], self.a["gdn_a_log"][l].rearrange("d (h o) -> (d h) o", o=1)).then_inc(small_in, 16)

                @block.tensor
                def _(pe):
                    pe.wait_ge(small_in, 48)
                    for half in range(2):
                        for k in range(KD):
                            if k % 2 == 0:
                                n = half * KD // 2 + k // 2
                                pe.wait_ge(squared, n + 1)
                                if n >= 2:
                                    pe.wait_ge(logged, n - 1)
                                for lo, hi in spans(0):
                                    last = pe.matmul(ps[:, 2 + n % 2, LC + lo:LC + hi], self.c("ones"), sq[:, n % 4, lo:hi], start=True, stop=True)
                                last.then_inc(squares_summed, 1)
                            for lo, hi in spans(0):
                                last = pe.matmul(ps[0:8, half, LC + lo:LC + hi], w[:, k, 8 * half:8 * half + 8],
                                                 self.hT[:, k, lo:hi], start=(k == 0), stop=(k == KD - 1))
                    last.then_inc(made, 1)
                    pe.wait_ge(flat, 1)
                    for t in range(TILES):
                        pe.transpose(ps[:, 0, 8 * t:8 * t + 8], betaT[:, t * P:(t + 1) * P], self.c("ident")[0:8, 0:8])
                        last = pe.transpose(ps[:, 0, 512 + 8 * t:512 + 8 * t + 8], gT[:, t * P:(t + 1) * P], self.c("ident")[0:8, 0:8])
                    last.then_inc(turned, 1)
                    pe.wait_ge(summed, 1)
                    for d, tri in enumerate(("upper", "lower")):
                        pe.matmul(ps[:, 1, d * 64:d * 64 + TILES * HEADS], self.c(tri), gn[:, d].rearrange("p t h -> p (t h)"), start=True, stop=True)
                        for t in range(TILES):
                            last = pe.matmul(ps[0:HEADS, d, LC + t * P:LC + (t + 1) * P], gn[:, d, t, :], self.c(tri), start=True, stop=True)
                    last.then_inc(turned, 1)

                @block.scalar
                def _(act):
                    step = Steps(act, own_act)
                    act.wait_ge(small_in, 48)

                    def square(n):
                        act.activation(sq[:, n % 4, :], qkvT[:, n, :], ACT.Square).then_inc(squared, 1)

                    step(act.activation(cols[:, 2:3], cols[:, 1:2], ACT.Exp))
                    square(0)
                    square(1)
                    for n in range(0, NU, 2):
                        for m in (n + 2, n + 3):
                            if m < NU:
                                if m >= 4:
                                    act.wait_ge(scaled, m - 3)
                                square(m)
                        for m in (n, n + 1):
                            scale, eps = (float(P), self.eps[:, 2:3]) if m < HEADS else (1.0, self.eps[:, 0:1])
                            act.wait_ge(squares_summed, m + 1)
                            act.activation(sq[:, m % 4, :], ps[:, 2 + m % 2, LC:], ACT.Ln, scale=scale, bias=eps).then_inc(logged, 1)
                        for m in (n, n + 1):
                            act.wait_ge(logged, m + 1)
                            act.activation(sq[:, m % 4, :], sq[:, m % 4, :], ACT.Exp, scale=-0.5).then_inc(inverted, 1)
                    act.wait_ge(made, 1)
                    step(act.activation(betaT[:, :], ps[0:8, 0, LC:], ACT.Sigmoid))
                    act.wait_ge(own, 1)
                    step(act.activation(ga[:, :], gx[:, :], ACT.Abs))
                    step.settle()
                    step(act.activation(ge[:, :], ga[:, :], ACT.Exp, scale=-1.0))
                    step.settle()
                    step(act.activation(gl[:, :], ge[:, :], ACT.Ln, bias=self.eps[0:8, 3:4]))
                    act.wait_ge(own, 7)
                    step(act.activation(eg[:, :, :], gc_nat[:, :, :], ACT.Exp))

                @block.vector
                def _(dve):
                    step = Steps(dve, own)
                    for n in range(NU):
                        dve.wait_ge(inverted, n + 1)
                        dve.tensor_tensor(qkvT[:, n, :], qkvT[:, n, :], sq[:, n % 4], ALU.mult).then_inc(scaled, 1)
                    dve.wait_ge(made, 1)
                    step(dve.tensor_scalar(gx[:, :], ps[0:8, 1, LC:], cols[:, 0:1], None, ALU.add))
                    dve.wait_ge(own_act, 5)
                    step.settle()
                    step(dve.scalar_tensor_tensor(gm[:, :], gx[:, :], 0.0, gl[:, :], ALU.max, ALU.add))
                    step.settle()
                    dve.tensor_scalar(gT[:, :], gm[:, :], cols[:, 2:3], -1.0, ALU.mult, ALU.mult).then_inc(flat, 1)
                    dve.wait_ge(turned, 1)
                    step(dve.tensor_copy(beta_nat[:, :, :], ps[:, 0, 0:8 * TILES].rearrange("p (t c) -> p t c", c=8)))
                    for d in range(2):
                        last = dve.tensor_copy(gn[:, d], ps[:, 0, 512:512 + 8 * TILES].rearrange("p (t c) -> p t c", c=8)[:, :, HEADS * d:HEADS * (d + 1)])
                    last.then_inc(summed, 1)
                    dve.wait_ge(turned, 2)
                    for d in range(2):
                        step(dve.tensor_copy(gcT[d][:, :], ps[0:HEADS, d, LC:]))
                    for d in range(2):
                        step(dve.tensor_copy(gc_nat[:, :, HEADS * d:HEADS * (d + 1)],
                                             ps[:, 1, d * 64:d * 64 + TILES * HEADS].rearrange("p (t h) -> p t h", h=HEADS)))
                    dve.wait_ge(own_act, 6)
                    dve.tensor_tensor(kscale[:, :, :], eg[:, :, :], beta_nat[:, :, :], ALU.mult)

    def gdn_scan(self, qkvT, oaT, betaT, gcT, beta_nat, gc_nat, kscale):
        nc, ps = self.nc, self.ps
        H4 = HEADS * P
        top = LEVELS - 1
        V_LAST = 5 + 3 * top
        T_LAST = 2 + 3 * top + 4
        A_LAST = 5
        with Stage(self) as s:
            t_done, v_done, a_done = s.signals(2), s.signals(2), s.signals(2)
            own, zeroed = s.signals(2)
            names = ("kT", "vT", "kb", "diff", "dec", "eg", "qd", "kd", "ke", "vb", "low", "qk", "W", "Wt", "X", "wT", "vn", "state")
            bufs = [{n: s.sb(f"{n}{d}", [P, H4]) for n in names} for d in range(2)]
            kds = [s.sb(f"kds{d}", [P, HEADS]) for d in range(2)]
            kde = [s.sb(f"kde{d}", [P, HEADS]) for d in range(2)]

            def bank(d, n):
                return ps[:, 2 * d + n // 2, 512 * (n % 2):512 * (n % 2) + H4]

            def heads(ap):
                return ap.rearrange("p (h c) -> p h c", h=HEADS)

            def hd(ap, h):
                return ap[:, h * P:(h + 1) * P]

            def mask(d, lv):
                return over(self.c("masks")[:, (d * LEVELS + lv) * P:(d * LEVELS + lv + 1) * P], HEADS)

            loops = ((0, CTILES, CTILES - 1), (CTILES, TILES, CTILES + TILES - 1))

            def tile(d, i, mirror):
                return i if d == 0 else (i * -1) + mirror

            with nc.Block() as block:
                @block.tensor
                def _(pe):
                    def four(out, lhs, rhs, start=True, stop=True):
                        for h in range(HEADS):
                            last = pe.matmul(hd(out, h), hd(lhs, h), hd(rhs, h), start=start, stop=stop)
                        return last

                    pe.wait_ge(zeroed, 1)
                    for first, end, mirror in loops:
                        with pe.Fori(first, end) as i:
                            for d, b in enumerate(bufs):
                                tok = bass.ts(tile(d, i, mirror), P)
                                pe.wait_ge(a_done[d], i * A_LAST + 1)
                                for h in range(HEADS):
                                    pe.transpose(hd(bank(d, 2), h), hd(b["kT"][:, :], h), self.c("ident"))
                                hold(pe, v_done[d], i * V_LAST + 1)
                                for h in range(HEADS):
                                    pe.transpose(hd(bank(d, 3), h), hd(b["vT"][:, :], h), self.c("ident"))
                                for h in range(HEADS):
                                    j = HEADS * d + h
                                    pe.matmul(hd(bank(d, 1), h), self.c("sel")[0:8, j * P:(j + 1) * P], betaT[:, tok], start=True, stop=True)
                                    last = pe.matmul(hd(bank(d, 0), h), self.c("sel")[0:HEADS, h * P:(h + 1) * P], gcT[d][:, tok], start=True, stop=True)
                                last.then_inc(t_done[d], 1)
                            for d, b in enumerate(bufs):
                                tok = bass.ts(tile(d, i, mirror), P)
                                pe.wait_ge(v_done[d], i * V_LAST + 3)
                                four(bank(d, 0), b["kT"][:, :], b["kb"][:, :])
                                for h in range(HEADS):
                                    last = pe.matmul(hd(bank(d, 1), h), hd(b["kT"][:, :], h), qkvT[:, h, tok], start=True, stop=True)
                                last.then_inc(t_done[d], 1)
                            for d, b in enumerate(bufs):
                                pe.wait_ge(v_done[d], i * V_LAST + 4)
                                four(bank(d, 2), b["low"][:, :], self.c("ident4")).then_inc(t_done[d], 1)
                            for lv in range(1, LEVELS):
                                for d, b in enumerate(bufs):
                                    pe.wait_ge(v_done[d], i * V_LAST + (1 + 3 * lv if lv > 1 else 5))
                                    four(bank(d, 2), b["low"][:, :], b["W"][:, :]).then_inc(t_done[d], 1)
                                for d, b in enumerate(bufs):
                                    pe.wait_ge(v_done[d], i * V_LAST + 3 + 3 * lv)
                                    if lv < top:
                                        four(bank(d, 3), b["Wt"][:, :], b["X"][:, :]).then_inc(t_done[d], 1)
                                    four(bank(d, 0), b["X"][:, :], b["Wt"][:, :]).then_inc(t_done[d], 1)
                            for d, b in enumerate(bufs):
                                pe.wait_ge(v_done[d], i * V_LAST + 4 + 3 * top)
                                four(bank(d, 1), b["ke"][:, :], b["Wt"][:, :]).then_inc(t_done[d], 1)
                            for d, b in enumerate(bufs):
                                pe.wait_ge(a_done[d], i * A_LAST + 4)
                                for h in range(HEADS):
                                    pe.matmul(hd(bank(d, 2), h), hd(b["Wt"][:, :], h), hd(b["vb"][:, :], h), start=True, stop=False)
                                    last = pe.matmul(hd(bank(d, 2), h), hd(b["wT"][:, :], h), hd(b["state"][:, :], h), start=False, stop=True)
                                last.then_inc(t_done[d], 1)
                            for d, b in enumerate(bufs):
                                pe.wait_ge(a_done[d], i * A_LAST + 5)
                                for h in range(HEADS):
                                    pe.matmul(hd(bank(d, 3), h), hd(b["state"][:, :], h), hd(b["qd"][:, :], h), start=True, stop=False)
                                    last = pe.matmul(hd(bank(d, 3), h), hd(b["vn"][:, :], h), hd(b["qk"][:, :], h), start=False, stop=True)
                                last.then_inc(t_done[d], 1)
                                four(bank(d, 0), b["kd"][:, :], b["vn"][:, :]).then_inc(t_done[d], 1)

                @block.scalar
                def _(act):
                    for first, end, mirror in loops:
                        with act.Fori(first, end) as i:
                            for d, b in enumerate(bufs):
                                tok = bass.ts(tile(d, i, mirror), P)
                                act.activation(heads(b["kT"][:, :]), qkvT[:, HEADS:2 * HEADS, tok], ACT.Copy)
                                act.activation(heads(b["vT"][:, :]), qkvT[:, 2 * HEADS:3 * HEADS, tok], ACT.Copy).then_inc(a_done[d], 1)
                            for d, b in enumerate(bufs):
                                act.wait_ge(t_done[d], i * T_LAST + 1)
                                act.activation(b["eg"][:, :], bank(d, 0), ACT.Exp).then_inc(a_done[d], 1)
                                act.wait_ge(v_done[d], i * V_LAST + 2)
                                act.activation(b["dec"][:, :], b["diff"][:, :], ACT.Exp)
                                act.activation(kde[d][:, :], kds[d][:, :], ACT.Exp).then_inc(a_done[d], 1)
                            for d, b in enumerate(bufs):
                                act.wait_ge(t_done[d], i * T_LAST + T_LAST - 3)
                                act.activation(b["wT"][:, :], bank(d, 1), ACT.Copy, scale=-1.0).then_inc(a_done[d], 1)
                            for d, b in enumerate(bufs):
                                act.wait_ge(t_done[d], i * T_LAST + T_LAST - 2)
                                act.activation(b["vn"][:, :], bank(d, 2), ACT.Copy).then_inc(a_done[d], 1)

                @block.vector
                def _(dve):
                    step = Steps(dve, own)
                    for d, b in enumerate(bufs):
                        step(dve.memset(b["state"][:, :], 0.0))
                    step(dve.memset(oaT[:, :, :], 0.0))
                    step.settle()
                    dve.sem_inc(zeroed, 1)
                    for first, end, mirror in loops:
                        with dve.Fori(first, end) as i:
                            step.loop((i - first) if first else i, 34)
                            for d in range(2):
                                dve.sem_inc(v_done[d], 1)
                            for d, b in enumerate(bufs):
                                t = tile(d, i, mirror)
                                lastcol = P - 1 if d == 0 else 0
                                hold(dve, t_done[d], i * T_LAST + 1)
                                hold(dve, a_done[d], i * A_LAST + 2)
                                for h in range(HEADS):
                                    step(dve.tensor_scalar(hd(b["diff"][:, :], h), hd(bank(d, 0), h), gc_nat[:, t, HEADS * d + h:HEADS * d + h + 1],
                                                           0.0, ALU.subtract, ALU.min))
                                dve.tensor_tensor(kds[d][:, :], heads(bank(d, 0))[:, :, lastcol], gc_nat[:, t, HEADS * d:HEADS * (d + 1)],
                                                  ALU.subtract).then_inc(v_done[d], 1)
                                dve.tensor_tensor(b["kb"][:, :], b["kT"][:, :], bank(d, 1), ALU.mult).then_inc(v_done[d], 1)
                            for d, b in enumerate(bufs):
                                t = tile(d, i, mirror)
                                mine = slice(HEADS * d, HEADS * (d + 1))
                                hold(dve, a_done[d], i * A_LAST + 3)
                                step(dve.tensor_tensor(heads(b["dec"][:, :]), heads(b["dec"][:, :]), over(self.c("lower" if d else "upper"), HEADS), ALU.mult))
                                step(dve.tensor_tensor(heads(b["kd"][:, :]), heads(bank(d, 2)), each(kde[d][:, :], P), ALU.mult))
                                step(dve.tensor_tensor(heads(b["ke"][:, :]), heads(bank(d, 2)), each(kscale[:, t, mine], P), ALU.mult))
                            for d, b in enumerate(bufs):
                                step.settle(back=3 * (1 - d))
                                hold(dve, t_done[d], i * T_LAST + 2)
                                step(dve.tensor_tensor(b["low"][:, :], bank(d, 0), b["dec"][:, :], ALU.mult))
                                step.settle()
                                step(dve.tensor_tensor(heads(b["X"][:, :]), heads(b["low"][:, :]), mask(1 - d, 0), ALU.mult))
                                step.settle()
                                dve.tensor_tensor(b["Wt"][:, :], self.c("ident4"), b["X"][:, :], ALU.subtract).then_inc(v_done[d], 1)
                            for d, b in enumerate(bufs):
                                t = tile(d, i, mirror)
                                step(dve.tensor_tensor(heads(b["vb"][:, :]), heads(bank(d, 3)), each(beta_nat[:, t, HEADS * d:HEADS * (d + 1)], P), ALU.mult))
                            for d, b in enumerate(bufs):
                                hold(dve, t_done[d], i * T_LAST + 3)
                                step(dve.tensor_tensor(heads(b["X"][:, :]), heads(bank(d, 2)), mask(d, 0), ALU.mult))
                                step.settle()
                                dve.tensor_tensor(b["W"][:, :], self.c("ident4"), b["X"][:, :], ALU.subtract).then_inc(v_done[d], 1)
                            for lv in range(1, LEVELS):
                                for d, b in enumerate(bufs):
                                    dve.wait_ge(t_done[d], i * T_LAST + 1 + 3 * lv)
                                    dve.tensor_tensor(heads(b["X"][:, :]), heads(bank(d, 2)), mask(d, lv), ALU.mult).then_inc(v_done[d], 1)
                                if lv == 1:
                                    for d, b in enumerate(bufs):
                                        step(dve.tensor_tensor(b["qk"][:, :], bank(d, 1), b["dec"][:, :], ALU.mult))
                                        step(dve.tensor_tensor(heads(b["qd"][:, :]), qkvT[:, 0:HEADS, bass.ts(tile(d, i, mirror), P)], heads(b["eg"][:, :]), ALU.mult))
                                for d, b in enumerate(bufs):
                                    if lv < top:
                                        dve.wait_ge(t_done[d], i * T_LAST + 2 + 3 * lv)
                                        dve.tensor_tensor(b["W"][:, :], b["W"][:, :], bank(d, 3), ALU.subtract).then_inc(v_done[d], 1)
                                    dve.wait_ge(t_done[d], i * T_LAST + (3 if lv < top else 2) + 3 * lv)
                                    dve.tensor_tensor(b["Wt"][:, :], b["Wt"][:, :], bank(d, 0), ALU.subtract).then_inc(v_done[d], 1)
                            for d, b in enumerate(bufs):
                                tok = bass.ts(tile(d, i, mirror), P)
                                lastcol = P - 1 if d == 0 else 0
                                hold(dve, t_done[d], i * T_LAST + T_LAST)
                                step(dve.tensor_tensor(oaT[:, :, tok], oaT[:, :, tok], heads(bank(d, 3)), ALU.add))
                                for h in range(HEADS):
                                    last = dve.scalar_tensor_tensor(hd(b["state"][:, :], h), hd(b["state"][:, :], h), hd(b["eg"][:, :], h)[:, lastcol:lastcol + 1],
                                                                    hd(bank(d, 0), h), ALU.mult, ALU.add)
                                    if h < HEADS - 1:
                                        step(last)
                                last.then_inc(v_done[d], 1)
                            step.end(end - first)

    def columns(self, l, parts, lo):
        nc, ps = self.nc, self.ps
        NB = 4
        with Stage(self) as s:
            loaded = s.signals(2)
            slot_free, block_done, ps_free = s.signals(3)
            w = s.sb("w", [P, 2, KD, 2 * P])
            with nc.Block() as block:
                @block.sync
                def _(sp):
                    for n, (col, func, dst, first) in enumerate(parts):
                        for j in range(2):
                            if n:
                                sp.wait_ge(slot_free, 2 * n + j - 1)
                            sp.dma_start(w[:, j], self.w_in(l, col + 2 * P * j, 2 * P)).then_inc(loaded[j], 16)

                @block.tensor
                def _(pe):
                    for n, (col, func, dst, first) in enumerate(parts):
                        for b in range(NB):
                            m = NB * n + b
                            pe.wait_ge(loaded[b // 2], 16 * (n + 1))
                            if m >= 4:
                                pe.wait_ge(ps_free, m - 3)
                            for k in range(KD):
                                for lo_, hi in spans(first):
                                    last = pe.matmul(ps[:, m % 4, LC + lo_:LC + hi], w[:, b // 2, k, (b % 2) * P:(b % 2 + 1) * P],
                                                     self.hT[:, k, lo_:hi], start=(k == 0), stop=(k == KD - 1))
                            last.then_inc(block_done, 1)
                            if b % 2:
                                pe.wait_ge(block_done, m + 1)
                                pe.sem_inc(slot_free, 1)

                @block.scalar
                def _(act):
                    for n, (col, func, dst, first) in enumerate(parts):
                        for b in range(NB):
                            m = NB * n + b
                            act.wait_ge(block_done, m + 1)
                            act.activation(dst[:, b, first:], ps[:, m % 4, LC + first:], func).then_inc(ps_free, 1)

    def values_and_norms(self, l, vda, vhat, lo, jobs):
        nc, ps = self.nc, self.ps
        W = HEADS * P
        first = lo // P
        units = [(0, t) for t in range(TILES)] + [(1, t) for t in range(first, TILES)]
        with Stage(self) as s:
            w_in, g_in, made, taken, squares, rooted, own_vector, finished = s.signals(8)
            squared, summed, logged, inverted = s.signals(4)
            w = s.sb("w", [P, KD, W])
            gb = s.sb("gb", [P, W])
            junk = s.sb("junk", [P, W])
            ss = s.sb("ss", [P, TILES])
            root = s.sb("root", [P, TILES])
            inv = s.sb("inv", [P, TILES])
            sq = s.sb("sq", [P, 2, T])
            rs = s.sb("rs", [P, T])
            ri = s.sb("ri", [P, 2, T])

            def bank(n):
                return ps[:, 2 + n % 4 // 2, 512 * (n % 2):512 * (n % 2) + W]

            with nc.Block() as block:
                @block.sync
                def _(sp):
                    sp.dma_start(w[:, :, :], self.w_in(l, C_DV, W)).then_inc(w_in, 16)
                    sp.dma_start(gb[:, :], self.a["cmlp_v_norm_g"][l].partition_broadcast(P)).then_inc(g_in, 16)
                    sp.wait_ge(made, TILES)
                    sp.dma_start(w[:, :, :], self.w_in(l, C_V, W)).then_inc(w_in, 16)

                @block.tensor
                def _(pe):
                    def job_sum(n):
                        src, b, ones, start, root_of, finish = jobs[n]
                        pe.wait_ge(squared, n + 1)
                        if n >= 2:
                            pe.wait_ge(logged, n - 1)
                        for x, y in spans(start):
                            last = pe.matmul(ps[:, n % 2, LC + x:LC + y], self.c(ones), sq[:, n % 2, x:y], start=True, stop=True)
                        last.then_inc(summed, 1)

                    for n, (which, t) in enumerate(units):
                        pe.wait_ge(w_in, 16 * (which + 1))
                        if n >= 4:
                            pe.wait_ge(taken, n - 3)
                        for k in range(KD):
                            last = pe.matmul(bank(n), self.hT[:, k, t * P:(t + 1) * P], w[:, k, :], start=(k == 0), stop=(k == KD - 1))
                        last.then_inc(made, 1)
                        if n < len(jobs):
                            job_sum(n)
                    for n in range(len(units), len(jobs)):
                        job_sum(n)

                @block.scalar
                def _(act):
                    def square(n):
                        src, b, ones, start, root_of, finish = jobs[n]
                        if n >= 2:
                            act.wait_ge(summed, n - 1)
                        act.activation(sq[:, n % 2, start:], src[:, b, start:], ACT.Square).then_inc(squared, 1)

                    def inverse_root(n):
                        src, b, ones, start, root_of, finish = jobs[n]
                        scale, eps = root_of(b)
                        act.wait_ge(summed, n + 1)
                        if n:
                            act.wait_ge(inverted, n)
                        act.activation(rs[:, start:], ps[:, n % 2, LC + start:], ACT.Ln, scale=scale, bias=eps).then_inc(logged, 1)
                        if n >= 2:
                            act.wait_ge(finished, n - 1)
                        act.wait_ge(logged, n + 1)
                        act.activation(ri[:, n % 2, start:], rs[:, start:], ACT.Exp, scale=-0.5).then_inc(inverted, 1)

                    square(0)
                    for n in range(max(len(units), len(jobs))):
                        if n + 1 < len(jobs):
                            square(n + 1)
                        if n < len(units):
                            which, t = units[n]
                            act.wait_ge(made, n + 1)
                            if which:
                                act.activation(vhat[:, t, :], bank(n), ACT.Gelu_apprx_tanh).then_inc(taken, 1)
                            else:
                                act.activation(vda[:, t, :], bank(n), ACT.Copy).then_inc(taken, 1)
                        if n < len(jobs):
                            inverse_root(n)
                    act.wait_ge(squares, TILES - first)
                    act.activation(root[:, first:], ss[:, first:], ACT.Sqrt, scale=1.0 / W, bias=self.eps[:, 0:1]).then_inc(rooted, 1)

                @block.vector
                def _(dve):
                    step = Steps(dve, own_vector)
                    done = 0
                    for n in range(max(len(units), len(jobs))):
                        if n < len(units) and units[n][0]:
                            t = units[n][1]
                            dve.wait_ge(taken, n + 1)
                            if done:
                                dve.wait_ge(squares, done)
                            dve.tensor_tensor_reduce(out=junk[:, :], in0=vhat[:, t, :], in1=vhat[:, t, :], scale=1.0, scalar=0.0,
                                                     op0=ALU.mult, op1=ALU.add, accum_out=ss[:, t:t + 1]).then_inc(squares, 1)
                            done += 1
                        if n < len(jobs):
                            dve.wait_ge(inverted, n + 1)
                            jobs[n][5](dve, step, jobs[n][1], ri[:, n % 2]).then_inc(finished, 1)
                    dve.wait_ge(rooted, 1)
                    dve.wait_ge(g_in, 16)
                    step(dve.reciprocal(inv[:, first:], root[:, first:]))
                    step.settle()
                    for t in range(first, TILES):
                        dve.scalar_tensor_tensor(vhat[:, t, :], vhat[:, t, :], inv[:, t:t + 1], gb[:, :], ALU.mult, ALU.mult)

    def chunk_mlp(self, l, ybT, vhat, lo):
        nc, ps = self.nc, self.ps
        W = HEADS * P
        first = lo // P
        with Stage(self) as s:
            in_, turned, flat, mixed, own, done = s.signals(6)
            ws = s.sb("ws", [P, HEADS, P])
            wsT = s.sb("wsT", [P, W])
            bs = s.sb("bs", [P, W])
            sv = s.sb("sv", [P, 2, W])
            with nc.Block() as block:
                @block.sync
                def _(sp):
                    sp.dma_start(ws[:, :, :], self.a["cmlp_w_s"][l].rearrange("g p q -> p g q")).then_inc(in_, 16)
                    sp.dma_start(bs[:, :], self.a["cmlp_b_s"][l].rearrange("g p -> (g p)").partition_broadcast(P)).then_inc(in_, 16)

                @block.tensor
                def _(pe):
                    pe.wait_ge(in_, 32)
                    for g in range(HEADS):
                        last = pe.transpose(ps[:, 3, g * P:(g + 1) * P], ws[:, g, :], self.c("ident"))
                    last.then_inc(turned, 1)
                    pe.wait_ge(flat, 1)
                    for t in range(first, TILES):
                        n = t - first
                        if n >= 2:
                            pe.wait_ge(done, n - 1)
                        for g in range(HEADS):
                            last = pe.matmul(ps[:, n % 2, g * P:(g + 1) * P], vhat[:, t, g * P:(g + 1) * P], wsT[:, g * P:(g + 1) * P], start=True, stop=True)
                        last.then_inc(mixed, 1)

                @block.vector
                def _(dve):
                    dve.wait_ge(turned, 1)
                    dve.tensor_copy(wsT[:, :], ps[:, 3, 0:W]).then_inc(flat, 1)
                    for t in range(first, TILES):
                        n = t - first
                        dve.wait_ge(mixed, n + 1)
                        dve.tensor_tensor(sv[:, n % 2], ps[:, n % 2, 0:W], bs[:, :], ALU.add).then_inc(own, 1)
                        dve.wait_ge(own, n + 1)
                        part = ybT[:, :, t * P:(t + 1) * P]
                        dve.tensor_tensor(part, part, sv[:, n % 2].rearrange("p (g c) -> p g c", g=HEADS), ALU.mult).then_inc(done, 1)

    def rotate(self, l, lam_init, qT, kT, lam):
        nc, ps = self.nc, self.ps
        with Stage(self) as s:
            swapped, own, done, lam_in, summed, spread, exps = s.signals(7)
            rot = s.sb("rot", [P, 2, LX])
            cosd = s.sb("cosd", [P, 2, LX])
            row = s.sb("row", [1, 4, DH])
            prod = s.sb("prod", [1, 2, DH])
            sums = s.sb("sums", [1, 2])
            el = s.sb("el", [P, 2])
            blocks = [(qT, h) for h in range(HEADS)] + [(kT, h) for h in range(HEADS)]
            with nc.Block() as block:
                @block.sync
                def _(sp):
                    sp.dma_start(row[:, :, :], self.a["da_lambda"][l:l + 1]).then_inc(lam_in, 16)

                @block.tensor
                def _(pe):
                    for n, (m, h) in enumerate(blocks):
                        if n >= 2:
                            pe.wait_ge(done, n - 1)
                        pe.matmul(ps[:, n % 2, 0:LX], self.c("perm"), m[:, h, LC:], start=True, stop=True).then_inc(swapped, 1)
                    pe.wait_ge(summed, 2)
                    pe.matmul(ps[:, 3, 0:2], self.c("ones")[0:1, :], sums[:, :], start=True, stop=True).then_inc(spread, 1)

                @block.scalar
                def _(act):
                    act.wait_ge(spread, 1)
                    act.activation(el[:, :], ps[:, 3, 0:2], ACT.Exp).then_inc(exps, 1)

                @block.vector
                def _(dve):
                    step = Steps(dve, own)
                    dve.wait_ge(lam_in, 16)
                    dve.tensor_tensor(prod[:, :, :], row[:, 0:4:2, :], row[:, 1:4:2, :], ALU.mult).then_inc(summed, 1)
                    dve.wait_ge(summed, 1)
                    dve.reduce_sum(sums[:, :], prod[:, :, :], axis=AX).then_inc(summed, 1)
                    for n, (m, h) in enumerate(blocks):
                        dve.wait_ge(swapped, n + 1)
                        step(dve.tensor_tensor(rot[:, n % 2], ps[:, n % 2, 0:LX], self.c("sin"), ALU.mult))
                        step(dve.tensor_tensor(cosd[:, n % 2], m[:, h, LC:], self.c("cos"), ALU.mult))
                        step.settle()
                        dve.tensor_tensor(m[:, h, LC:], cosd[:, n % 2], rot[:, n % 2], ALU.add).then_inc(done, 1)
                    dve.wait_ge(exps, 1)
                    dve.tensor_scalar(lam[:, :], el[:, 1:2], el[:, 0:1], -lam_init, ALU.subtract, ALU.add)

    def attend(self, qT, kT, vda, lam, oT, lo):
        nc, ps = self.nc, self.ps
        units = [(h, t) for h in range(HEADS) for t in range(lo // P, TILES)]
        NU = len(units)
        SCALE = DH ** -0.5
        with Stage(self) as s:
            scored, maxed, exped, mixed, turned, flat, valued, own = s.signals(8)
            p = s.sb("p", [P, 2, 2, T])
            a = s.sb("a", [P, 2, T])
            aT = s.sb("aT", [P, 2, T])
            mx = s.sb("mx", [P, 2, 2])
            nm = s.sb("nm", [P, 2, 2])
            sm = s.sb("sm", [P, 2, 2])
            r = s.sb("r", [P, 2, 2])
            rl = s.sb("rl", [P, 2])

            def keys(u):
                return LC if units[u][1] < CTILES else T

            def tokens(u):
                return slice(units[u][1] * P, (units[u][1] + 1) * P)

            def out(u):
                return ps[:, 3, 512 * (u % 2):512 * (u % 2) + P]

            with nc.Block() as block:
                @block.tensor
                def _(pe):
                    def scores(u, m):
                        h = units[u][0]
                        part = slice(DH * m, DH * (m + 1))
                        for b, e in spans(0)[:1 if keys(u) == LC else 2]:
                            last = pe.matmul(ps[:, m, LC + b:LC + e], qT[part, h, tokens(u)], kT[part, h, b:e], start=True, stop=True)
                        last.then_inc(scored, 1)

                    def values(u):
                        h, nk = units[u][0], keys(u) // P
                        pe.wait_ge(flat, u + 1)
                        for t in range(nk):
                            last = pe.matmul(out(u), vda[:, t, h * P:(h + 1) * P], aT[:, u % 2, t * P:(t + 1) * P], start=(t == 0), stop=(t == nk - 1))
                        last.then_inc(valued, 1)

                    scores(0, 0)
                    scores(0, 1)
                    for u in range(NU):
                        for m in range(2):
                            if u + 1 < NU:
                                pe.wait_ge(exped, 2 * u + m + 1)
                                scores(u + 1, m)
                        if u:
                            values(u - 1)
                        pe.wait_ge(mixed, u + 1)
                        for t in range(keys(u) // P):
                            last = pe.transpose(ps[:, 2, LC + t * P:LC + (t + 1) * P], a[:, u % 2, t * P:(t + 1) * P], self.c("ident"))
                        last.then_inc(turned, 1)
                    values(NU - 1)

                @block.scalar
                def _(act):
                    def store(u):
                        act.wait_ge(valued, u + 1)
                        act.activation(oT[:, units[u][0], tokens(u)], out(u), ACT.Copy)

                    def flatten(u):
                        act.wait_ge(turned, u + 1)
                        act.activation(aT[:, u % 2, 0:keys(u)], ps[:, 2, LC:LC + keys(u)], ACT.Copy).then_inc(flat, 1)

                    for u in range(NU):
                        for m in range(2):
                            act.wait_ge(maxed, 2 * u + m + 1)
                            act.activation(p[:, u % 2, m, 0:keys(u)], ps[:, m, LC:LC + keys(u)], ACT.Exp, scale=SCALE,
                                           bias=nm[:, u % 2, m:m + 1], accum_out=sm[:, u % 2, m:m + 1]).then_inc(exped, 1)
                        if u >= 1:
                            flatten(u - 1)
                        if u >= 2:
                            store(u - 2)
                    flatten(NU - 1)
                    store(NU - 2)
                    store(NU - 1)

                @block.vector
                def _(dve):
                    step = Steps(dve, own)

                    def maximum(u, m):
                        w = u % 2
                        dve.wait_ge(scored, 2 * u + m + 1)
                        step(dve.reduce_max(mx[:, w, m:m + 1], ps[:, m, LC:LC + keys(u)], axis=AX))
                        step.settle()
                        dve.tensor_scalar(nm[:, w, m:m + 1], mx[:, w, m:m + 1], -SCALE, None, ALU.mult).then_inc(maxed, 1)

                    maximum(0, 0)
                    maximum(0, 1)
                    for u in range(NU):
                        w, n = u % 2, keys(u)
                        if u + 1 < NU:
                            maximum(u + 1, 0)
                        dve.wait_ge(exped, 2 * u + 2)
                        step(dve.reciprocal(r[:, w], sm[:, w]))
                        step.settle()
                        step(dve.tensor_scalar(rl[:, w:w + 1], r[:, w, 1:2], lam[:, 0:1], None, ALU.mult))
                        step(dve.tensor_scalar(p[:, w, 0, 0:n], p[:, w, 0, 0:n], r[:, w, 0:1], None, ALU.mult))
                        step.settle()
                        dve.scalar_tensor_tensor(a[:, w, 0:n], p[:, w, 1, 0:n], rl[:, w:w + 1], p[:, w, 0, 0:n],
                                                 ALU.mult, ALU.add).then_inc(mixed, 1)
                        if u + 1 < NU:
                            maximum(u + 1, 1)

    def merge(self, l, out_scale, yaT, ybT, ycT, yT, lo):
        nc, ps = self.nc, self.ps
        HB = HEADS
        branches = (("w_branch_a", yaT), ("w_branch_b", ybT), ("w_branch_c", ycT))
        with Stage(self) as s:
            loaded = s.signals(2)
            slot_free, multiplied, opened, taken, own = s.signals(5)
            squared, summed, logged, inverted, normed = s.signals(5)
            sq = s.sb("sq", [P, HB, T])
            wg = s.sb("wg", [P, 2, 3, KD, P])
            wb = s.sb("wb", [P, 2, 3, HB, P])
            sg = s.sb("sg", [P, 2, T])
            part = s.sb("part", [P, 3, T])
            acc = s.sb("acc", [P, T])
            with nc.Block() as block:
                @block.sync
                def _(sp):
                    with sp.Fori(0, KD // 2) as i:
                        for j in range(2):
                            sp.wait_ge(slot_free, i * 2 + (j + 1))
                            for g, (name, _) in enumerate(branches):
                                sp.dma_start(wg[:, j, g], self.w_in(l, C_G + g * D, D)[:, :, bass.ts(i * 2 + j, P)]).then_inc(loaded[j], 16)
                                sp.dma_start(wb[:, j, g], self.a[name][l].rearrange("(k p) n -> p k n", p=P)[:, :, bass.ts(i * 2 + j, P)]).then_inc(loaded[j], 16)

                @block.tensor
                def _(pe):
                    pe.sem_inc(slot_free, 2)
                    pe.sem_inc(taken, 2)
                    for b in range(HB):
                        pe.wait_ge(squared, b + 1)
                        for x, y in spans(lo):
                            last = pe.matmul(ps[:, b, LC + x:LC + y], self.c("ones"), sq[:, b, x:y], start=True, stop=True)
                        last.then_inc(summed, 1)
                    pe.wait_ge(logged, HB)
                    with pe.Fori(0, KD // 2) as i:
                        for j in range(2):
                            pe.wait_ge(loaded[j], i * 96 + 96)
                            for g, (_, y) in enumerate(branches):
                                n = 3 * j + g
                                pe.wait_ge(taken, i * 6 + (n + 1))
                                pair = 2 * (n % 2)
                                for k in range(KD):
                                    for b, e in spans(lo):
                                        pe.matmul(ps[:, pair, LC + b:LC + e], wg[:, j, g, k, :], self.hT[:, k, b:e], start=(k == 0), stop=(k == KD - 1))
                                if g == 2:
                                    pe.wait_ge(normed, HB)
                                for k in range(HB):
                                    for b, e in spans(lo):
                                        last = pe.matmul(ps[:, pair + 1, LC + b:LC + e], wb[:, j, g, k, :], y[:, k, b:e], start=(k == 0), stop=(k == HB - 1))
                                last.then_inc(multiplied, 1)
                            pe.wait_ge(multiplied, i * 6 + (3 * j + 3))
                            pe.sem_inc(slot_free, 1)

                @block.scalar
                def _(act):
                    for b in range(HB):
                        act.activation(sq[:, b, lo:], ycT[:, b, lo:], ACT.Square).then_inc(squared, 1)
                    for b in range(HB):
                        act.wait_ge(summed, b + 1)
                        act.activation(sq[:, b, lo:], ps[:, b, LC + lo:], ACT.Ln, scale=1.0 / P / out_scale ** 2,
                                       bias=self.eps[:, 4 + l:5 + l]).then_inc(logged, 1)
                    for b in range(HB):
                        act.wait_ge(logged, b + 1)
                        act.activation(sq[:, b, lo:], sq[:, b, lo:], ACT.Exp, scale=-0.5).then_inc(inverted, 1)
                    with act.Fori(0, KD // 2) as i:
                        for n in range(6):
                            act.wait_ge(multiplied, i * 6 + (n + 1))
                            act.activation(sg[:, n % 2, lo:], ps[:, 2 * (n % 2), LC + lo:], ACT.Sigmoid).then_inc(opened, 1)

                @block.vector
                def _(dve):
                    step = Steps(dve, own)
                    for b in range(HB):
                        dve.wait_ge(inverted, b + 1)
                        dve.scalar_tensor_tensor(ycT[:, b, lo:], ycT[:, b, lo:], self.cols[:, 2:3], sq[:, b, lo:], ALU.mult, ALU.mult).then_inc(normed, 1)
                    with dve.Fori(0, KD // 2) as i:
                        step.loop(i, 4)
                        for j in range(2):
                            for g in range(3):
                                n = 3 * j + g
                                dve.wait_ge(opened, i * 6 + (n + 1))
                                dve.tensor_tensor(part[:, g, lo:], sg[:, n % 2, lo:], ps[:, 2 * (n % 2) + 1, LC + lo:], ALU.mult).then_inc(taken, 1)
                            dve.wait_ge(taken, i * 6 + (3 * j + 2 + 2))
                            step(dve.tensor_tensor(acc[:, lo:], part[:, 0, lo:], part[:, 1, lo:], ALU.add))
                            dve.wait_ge(taken, i * 6 + (3 * j + 3 + 2))
                            step.settle()
                            step(dve.tensor_tensor(yT[:, i * 2 + j, lo:], acc[:, lo:], part[:, 2, lo:], ALU.add))
                        step.end(KD // 2)

    def add_mixed(self, l, yT, lo):
        with Stage(self) as s:
            block_done, ps_free = s.signals(2)
            with self.nc.Block() as block:
                self.project(s, block, self.a["w_out"][l].rearrange("(k p) n -> p k n", p=P), yT, KD, lo, block_done, ps_free)

                @block.vector
                def _(dve):
                    with dve.Fori(0, KD // 2) as i:
                        for j in range(2):
                            dve.wait_ge(block_done, i * 2 + (j + 1))
                            for b, e, kind in KIND_RANGE:
                                if e > lo:
                                    last = dve.scalar_tensor_tensor(self.xT[:, i * 2 + j, b:e], self.ps[:, j, LC + b:LC + e],
                                                                    self.modT[:, i * 2 + (2 * KD + j), kind:kind + 1],
                                                                    self.xT[:, i * 2 + j, b:e], ALU.mult, ALU.add)
                            last.then_inc(ps_free, 1)

    def gain_finish(self, src, gain, lo):
        def finish(dve, step, b, r):
            return dve.scalar_tensor_tensor(src[:, b, lo:], src[:, b, lo:], gain, r[:, lo:], ALU.mult, ALU.mult)
        return finish

    def gated_finish(self, oaT, szT, lo):
        def finish(dve, step, b, r):
            step(dve.tensor_tensor(oaT[:, b, lo:], oaT[:, b, lo:], r[:, lo:], ALU.mult))
            step.settle()
            return dve.scalar_tensor_tensor(oaT[:, b, lo:], oaT[:, b, lo:], self.cols[:, 3:4], szT[:, b, lo:], ALU.mult, ALU.mult)
        return finish

    def mixers(self, l, lo):
        nc = self.nc
        lam_init = 0.8 - 0.6 * math.exp(-0.3 * l)
        with ExitStack() as outer:
            def sb(st, name, shape):
                return st.enter_context(nc.sbuf_tensor(f"{name}_{l}", shape, F32))
            oaT = sb(outer, "oaT", [P, HEADS, T])
            with ExitStack() as st:
                qkvT = sb(st, "qkvT", [P, 3 * HEADS, T])
                betaT = sb(st, "betaT", [2 * HEADS, T])
                gcT = [sb(st, f"gcT{d}", [HEADS, T]) for d in range(2)]
                beta_nat, gc_nat, kscale = (sb(st, n, [P, TILES, 2 * HEADS]) for n in ("beta_nat", "gc_nat", "kscale"))
                self.gdn_qkv(l, qkvT)
                self.gdn_gates(l, qkvT, betaT, gcT, beta_nat, gc_nat, kscale)
                self.gdn_scan(qkvT, oaT, betaT, gcT, beta_nat, gc_nat, kscale)
            ybT = sb(outer, "ybT", [P, HEADS, T])
            ycT = sb(outer, "ycT", [P, HEADS, T])
            with ExitStack() as st:
                szT, qT, kT = (sb(st, n, [P, HEADS, T]) for n in ("szT", "qT", "kT"))
                vda, vhat = (sb(st, n, [P, TILES, HEADS * P]) for n in ("vda", "vhat"))
                lam = sb(st, "lam", [P, 1])
                self.columns(l, ((C_Z, ACT.Silu, szT, lo), (C_U, ACT.Gelu_apprx_tanh, ybT, lo), (C_Q, ACT.Copy, qT, lo), (C_K, ACT.Copy, kT, 0)), lo)
                root = lambda b: (1.0 / DH, self.eps[:, 0:1])
                jobs = [(oaT, b, "ones", lo, lambda b: (1.0 / P, self.eps[:, 0:1]), self.gated_finish(oaT, szT, lo)) for b in range(HEADS)]
                jobs += [(qT, b, "blockones", lo, root, self.gain_finish(qT, self.cols[:, 0:1], lo)) for b in range(HEADS)]
                jobs += [(kT, b, "blockones", 0, root, self.gain_finish(kT, self.cols[:, 1:2], 0)) for b in range(HEADS)]
                self.values_and_norms(l, vda, vhat, lo, jobs)
                self.chunk_mlp(l, ybT, vhat, lo)
                self.rotate(l, lam_init, qT, kT, lam)
                self.attend(qT, kT, vda, lam, ycT, lo)
            yT = sb(outer, "yT", [P, KD, T])
            self.merge(l, 1.0 - lam_init, oaT, ybT, ycT, yT, lo)
            self.add_mixed(l, yT, lo)

    def peer_experts(self, l, qpT, picks, gates, lo):
        nc, ps = self.nc, self.ps
        NBATCH = PICKS // BATCH
        NB = 2 * PH
        NEG = -3.0e38
        CHOICE = 25
        VECTOR_SLOTS = (0, BATCH // 2)
        TENSOR_SLOTS = tuple(j for j in range(BATCH) if j not in VECTOR_SLOTS)
        OWN = NBATCH + 2
        first, last_tile = lo // P, TILES - 1
        half = NBATCH // 2
        assert half == PH and NBATCH * BATCH == PH * TOPK and TOPK == 2 * BATCH
        gathered, before = self.gathered, self.gathered_count
        self.gathered_count += 16 * 2 * NBATCH * (TILES - first)
        tables = (self.a["peer_u"], self.a["peer_v"])
        with Stage(self) as s:
            used = s.signals(BATCH)
            listed, h_copied, h_turned, h_ready, dotted, gelued, own, weighted = s.signals(8)
            copied_weights, diag_ready, acc_done, totalled, sum_copied, sum_turned, zeroed = s.signals(7)
            wq_in = s.signals(2)
            wq_free, multiplied, q_free = s.signals(3)
            keys_in, keys_turned, keys_ready, q_staged, scored, sc_ready, subtracted, exped, picked, chosen = s.signals(10)
            ring = s.sb("ring", [P, BATCH, D])
            ist = s.sb("ist", [P, 2, BATCH], U32)
            hs = s.sb("hs", [P, KD, P])
            hn = s.sb("hn", [P, KD, P])
            dots = s.sb("dots", [P, 2, BATCH])
            act_in = s.sb("act_in", [P, PICKS])
            act_out = s.sb("act_out", [P, PICKS])
            wgt = s.sb("wgt", [P, PICKS])
            wst = s.sb("wst", [P, 2, BATCH])
            diag = s.sb("diag", [P, 2, len(TENSOR_SLOTS), P])
            zero = s.sb("zero", [P, P])
            acc = s.sb("acc", [P, 2, D])
            accs = s.sb("accs", [P, D])
            kT = s.sb("kT", [P, NB, NKEYS])
            qs = s.sb("qs", [P, 2, P])
            sc = s.sb("sc", [P, 2, NKEYS])
            sc2 = s.sb("sc2", [P, 2, NKEYS])
            val = s.sb("val", [P, 2, TOPK])
            ix = s.sb("ix", [P, 2, TOPK], U32)
            ixf = s.sb("ixf", [P, 2, TOPK])
            cand = s.sb("cand", [P, TOPK * TOPK])
            cand2 = s.sb("cand2", [P, TOPK * TOPK])
            best = s.sb("best", [P, TOPK])
            pos = s.sb("pos", [P, TOPK], U32)
            side = s.sb("side", [P, 2, TOPK], U32)
            sidef = s.sb("sidef", [P, 2, TOPK])
            hot = s.sb("hot", [P, 2 * TOPK, TOPK])
            got = s.sb("got", [P, 2, TOPK])
            ex = s.sb("ex", [P, TOPK])
            tot = s.sb("tot", [P, 1])
            rt = s.sb("rt", [P, 1])
            kn = ring[:, 0:2, :].rearrange("p r (b c) -> p (r b) c", c=P)
            wq = ring[:, 4:8, :].rearrange("p (j r) (k c) -> p j (r k) c", j=2, c=2 * P)
            wq_src = self.a["peer_w_q"][l].rearrange("(k p) n -> p k n", p=P)
            ident = self.c("ident")

            def token_major(ap):
                return ap.rearrange("p k c -> p (k c)")

            def head_number(i, kb):
                return (i - first) * PH + kb

            loops = [(max(b // P, first), min(e // P, last_tile), kind, True) for b, e, kind in reversed(KIND_RANGE) if e // P > first]
            loops.append((last_tile, TILES, 0, False))

            with nc.Block() as block:
                @block.sync
                def _(sp):
                    sp.dma_start(kn, self.a["peer_subkeys"][l].rearrange("h i n d -> n (h i) d")).then_inc(keys_in, 16)
                    with sp.Fori(0, PH // 2) as n:
                        for j in range(2):
                            sp.wait_ge(wq_free, n * 2 + (j + 1))
                            sp.dma_start(wq[:, j], wq_src[:, :, bass.ts(n * 2 + j, 2 * P)]).then_inc(wq_in[j], 16)

                @block.gpsimd
                def _(pool):
                    for j in range(BATCH):
                        pool.sem_inc(used[j], 1)
                    pool.wait_ge(wq_free, PH + 2)
                    with pool.Fori(first, TILES) as i:
                        for part, table in enumerate(tables):
                            with pool.Fori(0, half) as kb:
                                if part == 0:
                                    hold(pool, picked, head_number(i, kb) + 1)
                                for h in range(2):
                                    batch = (i - first) * (2 * NBATCH) + kb * 2 + (part * NBATCH + h)
                                    pool.tensor_copy(ist[:, h], picks[:, i, bass.ts(kb * 2 + h, BATCH)]).then_inc(listed, 1)
                                    hold(pool, listed, batch + 1)
                                    for j in range(BATCH):
                                        hold(pool, used[j], batch + 1)
                                        pool.indirect_dma_start(out=ring[:, j, :], out_offset=None, in_=table.rearrange("l e d -> (l e) d"),
                                                                in_offset=bass.IndirectOffsetOnAxis(ap=ist[:, h, j:j + 1], axis=0),
                                                                element_offset=l * EXPERTS * D).then_inc(gathered[j], 16)

                @block.scalar
                def _(act):
                    def prepare(i):
                        act.activation(hs[:, :, :], self.hT[:, :, bass.ts(i, P)], ACT.Copy).then_inc(h_copied, 1)
                        act.wait_ge(h_turned, i - first + 1)
                        act.activation(token_major(hn[:, :, :]), ps[:, 0, :], ACT.Copy).then_inc(h_ready, 1)

                    def stage_queries(i, kb):
                        act.activation(qs[:, :, :], qpT[:, bass.ts(kb, 2), bass.ts(i, P)], ACT.Copy).then_inc(q_staged, 1)

                    def take_scores(i, kb):
                        act.wait_ge(scored, head_number(i, kb) + 1)
                        act.activation(sc[:, :, :], ps[:, 3, 0:2 * NKEYS].rearrange("p (s n) -> p s n", s=2), ACT.Copy).then_inc(sc_ready, 1)

                    def exponentials(i, kb):
                        act.wait_ge(subtracted, head_number(i, kb) + 1)
                        act.activation(ex[:, :], ex[:, :], ACT.Exp, accum_out=tot[:, 0:1]).then_inc(exped, 1)

                    def diagonals(i, kb, h):
                        n = (i - first) * NBATCH + kb * 2 + h
                        batch = (i - first) * (2 * NBATCH) + kb * 2 + (NBATCH + h)
                        hold(act, used[BATCH - 1], batch)
                        act.activation(wst[:, h], wgt[:, bass.ts(kb * 2 + h, BATCH)], ACT.Copy).then_inc(copied_weights, 1)
                        hold(act, copied_weights, n + 1)
                        for m, j in enumerate(TENSOR_SLOTS):
                            last = act.activation(diag[:, h, m], ident, ACT.Copy, scale=wst[:, h, j:j + 1])
                        last.then_inc(diag_ready, 1)

                    def tile(i, more):
                        act.wait_ge(dotted, i - first + 1)
                        act.activation(act_out[:, :], act_in[:, :], ACT.Gelu_apprx_tanh).then_inc(gelued, 1)
                        if more:
                            prepare(i + 1)
                        hold(act, weighted, i - first + 1)
                        with act.Fori(0, half) as kb:
                            if more:
                                stage_queries(i + 1, kb)
                            diagonals(i, kb, 0)
                            if more:
                                take_scores(i + 1, kb)
                            diagonals(i, kb, 1)
                            if more:
                                exponentials(i + 1, kb)
                        act.wait_ge(totalled, i - first + 1)
                        act.activation(accs[:, :], ps[:, 2, :], ACT.Copy).then_inc(sum_copied, 1)

                    act.wait_ge(keys_turned, 1)
                    for n in range(2):
                        last = act.activation(kT[:, 8 * n:8 * n + 8, :], ps[:, n].rearrange("p (b c) -> p b c", b=8), ACT.Copy)
                    last.then_inc(keys_ready, 1)

                    def take_queries(kb):
                        for m in range(2):
                            hold(act, multiplied, kb * 2 + (m + 1))
                            last = act.activation(qs[:, m], ps[:, m, LC + lo:LC + lo + P], ACT.Copy)
                            if m == 1:
                                last.then_inc(q_staged, 1)
                            act.activation(qpT[:, kb * 2 + m, lo:], ps[:, m, LC + lo:], ACT.Copy).then_inc(q_free, 1)

                    take_queries(0)
                    take_scores(first, 0)
                    with act.Fori(1, PH) as kb:
                        take_queries(kb)
                        exponentials(first, kb - 1)
                        take_scores(first, kb)
                    exponentials(first, PH - 1)
                    prepare(first)
                    with act.Fori(first, last_tile) as i:
                        tile(i, True)
                    tile(last_tile, False)

                @block.tensor
                def _(pe):
                    def turn_h(i):
                        pe.wait_ge(h_copied, i - first + 1)
                        for k in range(KD):
                            last = pe.transpose(ps[:, 0, k * P:(k + 1) * P], hs[:, k, :], ident)
                        last.then_inc(h_turned, 1)

                    def scores(i, kb):
                        hold(pe, q_staged, head_number(i, kb) + 1)
                        for m in range(2):
                            last = pe.matmul(ps[:, 3, m * NKEYS:(m + 1) * NKEYS], qs[:, m, :], kT[:, kb * 2 + m, :], start=True, stop=True)
                        last.then_inc(scored, 1)

                    def both_halves(lhs, rhs, start=False, stop=False):
                        for b in range(2):
                            last = pe.matmul(ps[:, 2, 512 * b:512 * (b + 1)], lhs, rhs[b], start=start, stop=stop)
                        return last

                    def split(ap):
                        return ap[:, 0:512], ap[:, 512:1024]

                    def tile(i, more):
                        if more:
                            turn_h(i + 1)
                        pe.wait_ge(sum_copied, i - first + 1)
                        both_halves(zero[:, :], (self.consts[:, 0:512],) * 2, start=True)
                        with pe.Fori(0, half) as kb:
                            if more:
                                scores(i + 1, kb)
                            for h in range(2):
                                n = (i - first) * NBATCH + kb * 2 + h
                                batch = (i - first) * (2 * NBATCH) + kb * 2 + (NBATCH + h)
                                hold(pe, diag_ready, n + 1)
                                for m, j in enumerate(TENSOR_SLOTS):
                                    pe.wait_ge(gathered[j], batch * 16 + (before + 16))
                                    both_halves(diag[:, h, m], split(ring[:, j])).then_inc(used[j], 1)
                        pe.wait_ge(acc_done, i - first + 1)
                        both_halves(ident, split(acc[:, 0]))
                        both_halves(ident, split(acc[:, 1]), stop=True).then_inc(totalled, 1)
                        pe.wait_ge(sum_copied, i - first + 2)
                        for k in range(KD):
                            last = pe.transpose(ps[:, 1, k * P:(k + 1) * P], accs[:, k * P:(k + 1) * P], ident)
                        last.then_inc(sum_turned, 1)

                    pe.sem_inc(sum_copied, 1)
                    pe.wait_ge(keys_in, 16)
                    for b in range(NB):
                        last = pe.transpose(ps[:, b // 8, (b % 8) * P:(b % 8 + 1) * P], kn[:, b, :], ident)
                    last.then_inc(keys_turned, 1)
                    pe.wait_ge(keys_ready, 1)
                    pe.wait_ge(zeroed, 1)
                    pe.sem_inc(wq_free, 2)
                    pe.sem_inc(q_free, 2)
                    with pe.Fori(0, PH // 2) as n:
                        for j in range(2):
                            pe.wait_ge(wq_in[j], n * 16 + 16)
                            for m in range(2):
                                pe.wait_ge(q_free, n * 4 + (2 * j + m + 1))
                                for k in range(KD):
                                    for b, e in spans(lo):
                                        last = pe.matmul(ps[:, m, LC + b:LC + e], wq[:, j, k, m * P:(m + 1) * P],
                                                         self.hT[:, k, b:e], start=(k == 0), stop=(k == KD - 1))
                                last.then_inc(multiplied, 1)
                            pe.wait_ge(multiplied, n * 4 + (2 * j + 2))
                            pe.sem_inc(wq_free, 1)
                            scores(first, n * 2 + j)
                    turn_h(first)
                    with pe.Fori(first, last_tile) as i:
                        tile(i, True)
                    tile(last_tile, False)

                @block.vector
                def _(dve):
                    step = Steps(dve, chosen)

                    def choose(i, kb):
                        step.begin(head_number(i, kb) * CHOICE)
                        hold(dve, sc_ready, head_number(i, kb) + 1)
                        for m in range(2):
                            step(dve.max(val[:, m, 0:8], sc[:, m, :]))
                        step.settle(apart=True)
                        for m in range(2):
                            step(dve.match_replace(sc2[:, m, :], val[:, m, 0:8], sc[:, m, :], NEG))
                        for m in range(2):
                            step(dve.max_index(ix[:, m, 0:8], val[:, m, 0:8], sc[:, m, :]))
                        step.settle(back=2, apart=True)
                        for m in range(2):
                            step(dve.max(val[:, m, 8:16], sc2[:, m, :]))
                        step.settle(apart=True)
                        for m in range(2):
                            step(dve.max_index(ix[:, m, 8:16], val[:, m, 8:16], sc2[:, m, :]))
                        step(dve.tensor_tensor(cand[:, :].rearrange("p (a b) -> p a b", a=TOPK), each(val[:, 0], TOPK), over(val[:, 1], TOPK), ALU.add))
                        step.settle(apart=True)
                        step(dve.tensor_copy(ixf[:, :, :], ix[:, :, :]))
                        step(dve.max(best[:, 0:8], cand[:, :]))
                        step.settle(apart=True)
                        step(dve.match_replace(cand2[:, :], best[:, 0:8], cand[:, :], NEG))
                        step(dve.max_index(pos[:, 0:8], best[:, 0:8], cand[:, :]))
                        step.settle(back=1, apart=True)
                        step(dve.max(best[:, 8:16], cand2[:, :]))
                        step.settle(apart=True)
                        step(dve.max_index(pos[:, 8:16], best[:, 8:16], cand2[:, :]))
                        dve.tensor_tensor(ex[:, :], best[:, :], best[:, 0:1].broadcast_to([P, TOPK]), ALU.subtract).then_inc(subtracted, 1)
                        step.settle()
                        step(dve.tensor_single_scalar(side[:, 0], pos[:, :], 4, ALU.logical_shift_right))
                        step(dve.tensor_single_scalar(side[:, 1], pos[:, :], 15, ALU.bitwise_and))
                        step.settle(apart=True)
                        step(dve.tensor_copy(sidef[:, :, :], side[:, :, :]))
                        step.settle()
                        step(dve.tensor_tensor(hot[:, :, :], each(sidef[:, :, :].rearrange("p m k -> p (m k)"), TOPK), over(self.c("iota"), 2 * TOPK), ALU.is_equal))
                        step.settle()
                        h4 = hot[:, :, :].rearrange("p (m k) n -> p m k n", m=2)
                        step(dve.tensor_tensor(h4, h4, ixf[:, :, :].rearrange("p m (o n) -> p m o n", o=1).broadcast_to([P, 2, TOPK, TOPK]), ALU.mult))
                        step.settle(apart=True)
                        step(dve.reduce_sum(got[:, :, :].rearrange("p m k -> p (m k)"), hot[:, :, :], axis=AX))
                        step.settle(apart=True)
                        dve.scalar_tensor_tensor(picks[:, i, bass.ts(kb, TOPK)], got[:, 0], float(NKEYS), got[:, 1], ALU.mult, ALU.add).then_inc(picked, 1)

                    def gate(i, kb):
                        hold(dve, exped, head_number(i, kb) + 1)
                        step(dve.reciprocal(rt[:, :], tot[:, :]))
                        step.settle(apart=True)
                        step(dve.tensor_tensor(gates[:, i, bass.ts(kb, TOPK)], ex[:, :], rt[:, 0:1].broadcast_to([P, TOPK]), ALU.mult))
                        assert step.n == CHOICE, step.n

                    def dot_batch(i, kb, h):
                        batch = (i - first) * (2 * NBATCH) + kb * 2 + h
                        for j in range(BATCH):
                            dve.wait_ge(gathered[j], batch * 16 + (before + 16))
                            dve.tensor_tensor_reduce(out=ring[:, j, :], in0=ring[:, j, :], in1=token_major(hn[:, :, :]), scale=1.0, scalar=0.0,
                                                     op0=ALU.mult, op1=ALU.add, accum_out=dots[:, h, j:j + 1]).then_inc(used[j], 1)
                        hold(dve, used[BATCH - 1], batch + 2)
                        dve.tensor_copy(act_in[:, bass.ts(kb * 2 + h, BATCH)], dots[:, h]).then_inc(own, 1)

                    def sum_batch(i, kb, h):
                        batch = (i - first) * (2 * NBATCH) + kb * 2 + (NBATCH + h)
                        for n, j in enumerate(VECTOR_SLOTS):
                            dve.wait_ge(gathered[j], batch * 16 + (before + 16))
                            a = acc[:, n]
                            dve.scalar_tensor_tensor(a, ring[:, j, :], wgt[:, :].rearrange("p (b j) -> p b j", j=BATCH)[:, kb * 2 + h, j:j + 1],
                                                     a, ALU.mult, ALU.add).then_inc(used[j], 1)

                    dve.memset(zero[:, :], 0.0).then_inc(zeroed, 1)
                    with dve.Fori(0, PH) as kb:
                        choose(first, kb)
                        gate(first, kb)
                    for begin, end, kind, more in loops:
                        with dve.Fori(begin, end) as i:
                            hold(dve, h_ready, i - first + 1)
                            with dve.Fori(0, half) as kb:
                                for h in range(2):
                                    dot_batch(i, kb, h)
                            hold(dve, own, (i - first) * OWN + NBATCH)
                            dve.sem_inc(dotted, 1)
                            dve.memset(acc[:, :, :], 0.0).then_inc(own, 1)
                            hold(dve, chosen, (i - first) * (PH * CHOICE) + PH * CHOICE)
                            hold(dve, gelued, i - first + 1)
                            dve.tensor_tensor(wgt[:, :], act_out[:, :], gates[:, i, :], ALU.mult).then_inc(weighted, 1)
                            hold(dve, own, (i - first) * OWN + (NBATCH + 1))
                            hold(dve, weighted, i - first + 1)
                            with dve.Fori(0, half) as kb:
                                sum_batch(i, kb, 0)
                                if more:
                                    choose(i + 1, kb)
                                sum_batch(i, kb, 1)
                                if more:
                                    gate(i + 1, kb)
                            for j in VECTOR_SLOTS:
                                hold(dve, used[j], (i - first) * (2 * NBATCH) + (2 * NBATCH + 1))
                            dve.sem_inc(acc_done, 1)
                            hold(dve, sum_turned, i - first + 1)
                            tmp = accs[:, :].rearrange("p (k c) -> p k c", k=KD)
                            dve.tensor_tensor(tmp, ps[:, 1, :].rearrange("p (k c) -> p k c", k=KD),
                                              each(self.modT[:, 5 * KD:6 * KD, kind], P), ALU.mult).then_inc(own, 1)
                            hold(dve, own, (i - first) * OWN + OWN)
                            x_tile = self.xT[:, :, bass.ts(i, P)]
                            dve.tensor_tensor(x_tile, x_tile, tmp, ALU.add)

    def experts(self, l, lo):
        with ExitStack() as st:
            def sb(name, shape, dt=F32):
                return st.enter_context(self.nc.sbuf_tensor(f"{name}_{l}", shape, dt))
            picks = sb("picks", [P, TILES, PICKS], U32)
            gates = sb("gates", [P, TILES, PICKS])
            qpT = sb("qpT", [P, 2 * PH, T])
            self.peer_experts(l, qpT, picks, gates, lo)

    def store(self):
        nc, ps = self.nc, self.ps
        with Stage(self) as s:
            turned, flat, stored = s.signals(3)
            xn = s.sb("xn", [P, TILES - CTILES, D])
            with nc.Block() as block:
                @block.tensor
                def _(pe):
                    for t in range(TILES - CTILES):
                        for k in range(KD):
                            last = pe.transpose(ps[:, t, k * P:(k + 1) * P], self.xT[:, k, LC + t * P:LC + (t + 1) * P], self.c("ident"))
                        last.then_inc(turned, 1)

                @block.vector
                def _(dve):
                    for t in range(TILES - CTILES):
                        dve.wait_ge(turned, t + 1)
                        dve.tensor_copy(xn[:, t, :], ps[:, t, :]).then_inc(flat, 1)

                @block.sync
                def _(sp):
                    for t in range(TILES - CTILES):
                        sp.wait_ge(flat, t + 1)
                        sp.dma_start(self.out[0, t * P:(t + 1) * P, :], xn[:, t, :]).then_inc(stored, 16)
                    sp.wait_ge(stored, 16 * (TILES - CTILES))


def hybrid_kernel(nc, a, out):
    with ExitStack() as st:
        k = Kernel(nc, a, out, st)
        k.setup()
        for l in range(DEPTH):
            lo = LC if l == DEPTH - 1 else 0
            k.modulation(l)
            k.norm(k.gain1, 0, ready=True)
            k.mixers(l, lo)
            k.norm(k.gain2, 3, lo)
            k.experts(l, lo)
        k.store()


def kernel(**inputs):
    import concourse.bacc as bacc
    from concourse.bass_utils import run_bass_kernel_spmd

    nc = bacc.Bacc("TRN2", target_bir_lowering=False, num_devices=1)
    arrays = {name: np.ascontiguousarray(value) for name, value in inputs.items()}
    a = {name: nc.dram_tensor(name, value.shape, mybir.dt.from_np(value.dtype), kind="ExternalInput").ap()
         for name, value in arrays.items()}
    out = nc.dram_tensor("out", arrays["x"].shape, F32, kind="ExternalOutput").ap()
    hybrid_kernel(nc, a, out)
    return run_bass_kernel_spmd(nc, [arrays], core_ids=[0]).results[0]["out"]
```
